# Optimizing a Trainium2 kernel written in Bass

```python
import jax, jax.numpy as jnp
from jax import lax
import numpy as np

D_MODEL = 1024
BATCH = 1
SEQ = 256
DEPTH = 2

HEAD_DIM = 64
ROPE_THETA = 10000.0
LN_EPS = 1e-5
A_HEADS = 8
IDX_HEADS = 8
IDX_DIM = 32
DSA_TOPK = 256
DSA_QBLOCK = 128
B_HEADS = 8
B_GROUPS = ((128, 1), (512, 4), (2048, 16))
B_QBLOCK = 128
C_HEADS = 8
MOBA_BLOCK = 256
MOBA_TOPK = 3
MOBA_QCHUNK = 32
N_EXPERTS = 64
N_GROUPS = 8
TOPK_GROUPS = 4
TOP_K = 8
EXPERT_DIM = 256
SHARED_DIM = 256
ROUTED_SCALE = 2.5
ALPHA = (2 * DEPTH) ** 0.25
BETA = (8 * DEPTH) ** -0.25
IN_WIDTHS = (A_HEADS * HEAD_DIM, HEAD_DIM, HEAD_DIM, IDX_HEADS * IDX_DIM, IDX_DIM, IDX_HEADS,
             B_HEADS * HEAD_DIM, B_HEADS * HEAD_DIM, B_HEADS * HEAD_DIM,
             C_HEADS * HEAD_DIM, C_HEADS * HEAD_DIM, C_HEADS * HEAD_DIM,
             D_MODEL, D_MODEL, D_MODEL)
IN_WIDTH = sum(IN_WIDTHS)

kernel_name = 'hybrid_dsa_dilated_moba_moe_block'

F32 = jnp.float32

def layer_norm(x, g, b):
    xf = x.astype(F32)
    mu = xf.mean(-1, keepdims=True)
    var = jnp.mean(jnp.square(xf - mu), -1, keepdims=True)
    return ((xf - mu) * lax.rsqrt(var + LN_EPS) * g.astype(F32) + b.astype(F32)).astype(x.dtype)

def rope_tables(seq, dim):
    inv = ROPE_THETA ** (-jnp.arange(0, dim, 2, dtype=F32) / dim)
    ang = jnp.arange(seq, dtype=F32)[:, None] * inv[None, :]
    return jnp.cos(ang), jnp.sin(ang)

def apply_rope(x, cos, sin):
    extra = x.ndim - 3
    cos = cos.reshape(cos.shape[:1] + (1,) * extra + cos.shape[1:])
    sin = sin.reshape(sin.shape[:1] + (1,) * extra + sin.shape[1:])
    x1, x2 = jnp.split(x.astype(F32), 2, axis=-1)
    return jnp.concatenate([x1 * cos - x2 * sin, x2 * cos + x1 * sin], -1).astype(x.dtype)

def dsa_attention(q, k, v, qi, ki, wi):
    bsz, S, _, dh = q.shape
    topk = min(DSA_TOPK, S // 4)
    kpos = jnp.arange(S)
    def block(i):
        t0 = i * DSA_QBLOCK
        tq = t0 + jnp.arange(DSA_QBLOCK)
        qb = lax.dynamic_slice_in_dim(q, t0, DSA_QBLOCK, axis=1)
        qib = lax.dynamic_slice_in_dim(qi, t0, DSA_QBLOCK, axis=1)
        wib = lax.dynamic_slice_in_dim(wi, t0, DSA_QBLOCK, axis=1).astype(F32) * IDX_HEADS ** -0.5
        dots = jnp.einsum('bqhe,bse->bhqs', qib, ki, preferred_element_type=F32) * IDX_DIM ** -0.5
        score = jnp.einsum('bqh,bhqs->bqs', wib, jax.nn.relu(dots))
        causal = kpos[None, :] <= tq[:, None]
        score = jnp.where(causal[None], score, -jnp.inf)
        _, idx = lax.top_k(score, topk)
        valid = idx <= tq[None, :, None]
        kg = jax.vmap(lambda kk, ii: kk[ii])(k, idx)
        vg = jax.vmap(lambda vv, ii: vv[ii])(v, idx)
        logits = jnp.einsum('bqhd,bqkd->bhqk', qb, kg, preferred_element_type=F32) * dh ** -0.5
        logits = jnp.where(valid[:, None], logits, -jnp.inf)
        p = jax.nn.softmax(logits, axis=-1).astype(v.dtype)
        return jnp.einsum('bhqk,bqkd->bqhd', p, vg)
    out = lax.map(block, jnp.arange(S // DSA_QBLOCK))
    return jnp.moveaxis(out, 0, 1).reshape(bsz, S, -1)

def dilated_attention(q, k, v):
    bsz, S, H, dh = q.shape
    scale = dh ** -0.5
    def block(i):
        t0 = i * B_QBLOCK
        tq = t0 + jnp.arange(B_QBLOCK)
        qb = lax.dynamic_slice_in_dim(q, t0, B_QBLOCK, axis=1)
        ms, ls, outs = [], [], []
        for window, dil in B_GROUPS:
            n_keys = window // dil + 1
            kpos = tq[:, None] - dil * jnp.arange(n_keys)[None, :]
            valid = kpos >= 0
            kpos = jnp.maximum(kpos, 0)
            kg = k[:, kpos]
            vg = v[:, kpos]
            logits = jnp.einsum('bqhd,bqnhd->bhqn', qb, kg, preferred_element_type=F32) * scale
            logits = jnp.where(valid[None, None], logits, -jnp.inf)
            m = logits.max(-1)
            e = jnp.exp(logits - m[..., None])
            l = e.sum(-1)
            o = jnp.einsum('bhqn,bqnhd->bhqd', (e / l[..., None]).astype(v.dtype), vg,
                           preferred_element_type=F32)
            ms.append(m); ls.append(l); outs.append(o)
        m_all, l_all, o_all = jnp.stack(ms), jnp.stack(ls), jnp.stack(outs)
        wgt = l_all * jnp.exp(m_all - m_all.max(0))
        o = (wgt[..., None] * o_all).sum(0) / wgt.sum(0)[..., None]
        return o.transpose(0, 2, 1, 3).astype(q.dtype)
    out = lax.map(block, jnp.arange(S // B_QBLOCK))
    return jnp.moveaxis(out, 0, 1).reshape(bsz, S, -1)

def moba_attention(q, k, v):
    bsz, S, H, dh = q.shape
    scale = dh ** -0.5
    n_blk = -(-S // MOBA_BLOCK)
    pad = n_blk * MOBA_BLOCK - S
    k_pad = jnp.pad(k, ((0, 0), (0, pad), (0, 0), (0, 0)))
    v_pad = jnp.pad(v, ((0, 0), (0, pad), (0, 0), (0, 0)))
    k_blk = k_pad.reshape(bsz, n_blk, MOBA_BLOCK, H, dh).transpose(0, 3, 1, 2, 4)
    v_blk = v_pad.reshape(bsz, n_blk, MOBA_BLOCK, H, dh).transpose(0, 3, 1, 2, 4)
    k_mean = k_blk.astype(F32).mean(3)
    n_sel = max(1, min(MOBA_TOPK, n_blk - 1))
    b_ix = jnp.arange(bsz)[:, None, None, None]
    h_ix = jnp.arange(H)[None, :, None, None]
    blk_ids = jnp.arange(n_blk)
    def chunk(i):
        t0 = i * MOBA_QCHUNK
        tq = t0 + jnp.arange(MOBA_QCHUNK)
        own = t0 // MOBA_BLOCK
        qc = lax.dynamic_slice_in_dim(q, t0, MOBA_QCHUNK, axis=1)
        gate = jnp.einsum('bqhd,bhnd->bhqn', qc.astype(F32), k_mean)
        gate = jnp.where(blk_ids < own, gate, -jnp.inf)
        _, sel = lax.top_k(gate, n_sel)
        sel_ok = sel < own
        kg = k_blk[b_ix, h_ix, sel]
        vg = v_blk[b_ix, h_ix, sel]
        lp = jnp.einsum('bqhd,bhqkjd->bhqkj', qc, kg, preferred_element_type=F32) * scale
        lp = jnp.where(sel_ok[..., None], lp, -jnp.inf).reshape(bsz, H, MOBA_QCHUNK, n_sel * MOBA_BLOCK)
        start = own * MOBA_BLOCK
        k_own = lax.dynamic_slice_in_dim(k_pad, start, MOBA_BLOCK, axis=1)
        v_own = lax.dynamic_slice_in_dim(v_pad, start, MOBA_BLOCK, axis=1)
        lo = jnp.einsum('bqhd,bjhd->bhqj', qc, k_own, preferred_element_type=F32) * scale
        causal = (start + jnp.arange(MOBA_BLOCK))[None, :] <= tq[:, None]
        lo = jnp.where(causal, lo, -jnp.inf)
        p = jax.nn.softmax(jnp.concatenate([lp, lo], -1), axis=-1).astype(v.dtype)
        p_sel = p[..., :n_sel * MOBA_BLOCK].reshape(bsz, H, MOBA_QCHUNK, n_sel, MOBA_BLOCK)
        p_own = p[..., n_sel * MOBA_BLOCK:]
        return (jnp.einsum('bhqkj,bhqkjd->bqhd', p_sel, vg)
                + jnp.einsum('bhqj,bjhd->bqhd', p_own, v_own))
    out = lax.map(chunk, jnp.arange(S // MOBA_QCHUNK))
    return jnp.moveaxis(out, 0, 1).reshape(bsz, S, -1)

def token_mixing(u, w_in, ik_g, ik_b, w_br_a, w_br_b, w_br_c, w_out):
    bsz, S, _ = u.shape
    cos_h, sin_h = rope_tables(S, HEAD_DIM)
    cos_i, sin_i = rope_tables(S, IDX_DIM)
    proj = jnp.einsum('bsd,dn->bsn', u, w_in)
    parts = jnp.split(proj, np.cumsum(IN_WIDTHS)[:-1].tolist(), axis=-1)
    qa, ka, va, qi, ki, wi, qb, kb, vb, qc, kc, vc, ga, gb, gc = parts
    heads = lambda t, h: t.reshape(bsz, S, h, -1)
    qa = apply_rope(heads(qa, A_HEADS), cos_h, sin_h)
    ka = apply_rope(ka, cos_h, sin_h)
    qi = apply_rope(heads(qi, IDX_HEADS), cos_i, sin_i)
    ki = apply_rope(layer_norm(ki, ik_g, ik_b), cos_i, sin_i)
    o_a = dsa_attention(qa, ka, va, qi, ki, wi)
    o_b = dilated_attention(apply_rope(heads(qb, B_HEADS), cos_h, sin_h),
                            apply_rope(heads(kb, B_HEADS), cos_h, sin_h), heads(vb, B_HEADS))
    o_c = moba_attention(apply_rope(heads(qc, C_HEADS), cos_h, sin_h),
                         apply_rope(heads(kc, C_HEADS), cos_h, sin_h), heads(vc, C_HEADS))
    merged = (jax.nn.sigmoid(ga) * jnp.einsum('bsk,kd->bsd', o_a, w_br_a)
              + jax.nn.sigmoid(gb) * jnp.einsum('bsk,kd->bsd', o_b, w_br_b)
              + jax.nn.sigmoid(gc) * jnp.einsum('bsk,kd->bsd', o_c, w_br_c))
    return jnp.einsum('bsd,de->bse', merged, w_out)

def moe_ffn(u, w_router, router_bias, w_gate, w_up, w_down, ws_gate, ws_up, ws_down):
    bsz, S, _ = u.shape
    scores = jax.nn.sigmoid(jnp.einsum('bsd,de->bse', u, w_router, preferred_element_type=F32))
    biased = scores + router_bias.astype(F32)
    grp = biased.reshape(bsz, S, N_GROUPS, N_EXPERTS // N_GROUPS)
    grp_score = lax.top_k(grp, 2)[0].sum(-1)
    _, gidx = lax.top_k(grp_score, TOPK_GROUPS)
    gmask = jax.nn.one_hot(gidx, N_GROUPS, dtype=F32).sum(-2) > 0
    emask = jnp.repeat(gmask, N_EXPERTS // N_GROUPS, axis=-1)
    _, eidx = lax.top_k(jnp.where(emask, biased, -jnp.inf), TOP_K)
    w = jnp.take_along_axis(scores, eidx, -1)
    w = w / w.sum(-1, keepdims=True) * ROUTED_SCALE
    gates = (jax.nn.one_hot(eidx, N_EXPERTS, dtype=F32) * w[..., None]).sum(-2)
    def per_seq(args):
        us, gs = args
        h = (jax.nn.silu(jnp.einsum('sd,edf->sef', us, w_gate))
             * jnp.einsum('sd,edf->sef', us, w_up)) * gs[..., None].astype(us.dtype)
        return jnp.einsum('sef,efd->sd', h, w_down)
    routed = lax.map(per_seq, (u, gates))
    shared = jnp.einsum('bsf,fd->bsd', jax.nn.silu(jnp.einsum('bsd,df->bsf', u, ws_gate))
                        * jnp.einsum('bsd,df->bsf', u, ws_up), ws_down)
    return routed + shared

def setup_inputs(seed: int = 0) -> dict:
    key = jax.random.key(seed)
    ks = jax.random.split(key, 24)
    D, L = D_MODEL, DEPTH
    nrm = lambda k, shape, s: jax.random.normal(k, shape, F32) * s
    return {
        'x': nrm(ks[0], (BATCH, SEQ, D), 1.0),
        'c': nrm(ks[1], (BATCH, D), 1.0),
        'ada_w': nrm(ks[2], (L, D, 6 * D), 0.1 * D ** -0.5),
        'ada_b': nrm(ks[3], (L, 6 * D), 0.01),
        'w_in': nrm(ks[4], (L, D, IN_WIDTH), D ** -0.5),
        'ik_norm_g': 1.0 + nrm(ks[5], (L, IDX_DIM), 0.02),
        'ik_norm_b': nrm(ks[6], (L, IDX_DIM), 0.02),
        'w_br_a': nrm(ks[7], (L, A_HEADS * HEAD_DIM, D), (A_HEADS * HEAD_DIM) ** -0.5),
        'w_br_b': nrm(ks[8], (L, B_HEADS * HEAD_DIM, D), (B_HEADS * HEAD_DIM) ** -0.5),
        'w_br_c': nrm(ks[9], (L, C_HEADS * HEAD_DIM, D), (C_HEADS * HEAD_DIM) ** -0.5),
        'w_out': nrm(ks[10], (L, D, D), BETA * D ** -0.5),
        'ln1_g': 1.0 + nrm(ks[11], (L, D), 0.02),
        'ln1_b': nrm(ks[12], (L, D), 0.02),
        'w_router': nrm(ks[13], (L, D, N_EXPERTS), D ** -0.5),
        'router_bias': nrm(ks[14], (L, N_EXPERTS), 0.01),
        'w_gate': nrm(ks[15], (L, N_EXPERTS, D, EXPERT_DIM), D ** -0.5),
        'w_up': nrm(ks[16], (L, N_EXPERTS, D, EXPERT_DIM), D ** -0.5),
        'w_down': nrm(ks[17], (L, N_EXPERTS, EXPERT_DIM, D), BETA * EXPERT_DIM ** -0.5),
        'ws_gate': nrm(ks[18], (L, D, SHARED_DIM), D ** -0.5),
        'ws_up': nrm(ks[19], (L, D, SHARED_DIM), D ** -0.5),
        'ws_down': nrm(ks[20], (L, SHARED_DIM, D), BETA * SHARED_DIM ** -0.5),
        'ln2_g': 1.0 + nrm(ks[21], (L, D), 0.02),
        'ln2_b': nrm(ks[22], (L, D), 0.02),
    }

def reference(x, c, ada_w, ada_b, w_in, ik_norm_g, ik_norm_b, w_br_a, w_br_b, w_br_c, w_out,
              ln1_g, ln1_b, w_router, router_bias, w_gate, w_up, w_down, ws_gate, ws_up, ws_down,
              ln2_g, ln2_b):
    for l in range(DEPTH):
        mod = jnp.einsum('bd,dn->bn', jax.nn.silu(c), ada_w[l]) + ada_b[l]
        sh1, sc1, g1, sh2, sc2, g2 = jnp.split(mod[:, None, :], 6, axis=-1)
        u = x * (1 + sc1) + sh1
        y = token_mixing(u, w_in[l], ik_norm_g[l], ik_norm_b[l], w_br_a[l], w_br_b[l], w_br_c[l], w_out[l])
        x = layer_norm(ALPHA * x + (1 + g1) * y, ln1_g[l], ln1_b[l])
        u = x * (1 + sc2) + sh2
        y = moe_ffn(u, w_router[l], router_bias[l], w_gate[l], w_up[l], w_down[l],
                    ws_gate[l], ws_up[l], ws_down[l])
        x = layer_norm(ALPHA * x + (1 + g2) * y, ln2_g[l], ln2_b[l])
    return x


_drawn_inputs = setup_inputs


def setup_inputs(seed=0):
    import zlib

    import numpy as np

    out = dict(_drawn_inputs(seed))
    spreads = {}
    factors = {}
    for name, (base, spread) in spreads.items():
        noise = np.random.default_rng([zlib.crc32(name.encode()), seed]).standard_normal(out[name].shape)
        drawn = base * np.exp(spread * noise) if base else spread * noise
        out[name] = __import__('jax').numpy.asarray(drawn.astype(out[name].dtype))
    for name, factor in factors.items():
        out[name] = (out[name] * factor).astype(out[name].dtype)
    return out
```

```python
from contextlib import ExitStack

import concourse.bass as bass
from concourse import mybir

F32 = mybir.dt.float32
ALU = mybir.AluOpType
ACT = mybir.ActivationFunctionType
AX = mybir.AxisListType

P = 128
NEG = -1.0e30
SELECTED = -5.0e29


def build(nc, x, cT, ada_w, adaT_b, ada_b, w_in, ik_gb, w_br_a, w_br_b, w_br_c, w_out, ln_gb,
          w_router, router_bias, w_gate, w_up, w_down, ws_gate, ws_up, ws_down,
          ident_c, perm_c, rope_c, ropei_tok_c, mask_c, out):
    L, D, WIN = w_in.shape
    S = x.shape[0]
    E, F = w_gate.shape[1], w_gate.shape[3]
    DH, IH, ID = 64, 8, 32
    KD = D // P
    KF = F // P
    NT = S // P
    SC = 512
    HC = 3 * 8
    TOPK_ROUNDS = 64 // 8
    ALPHA = float((2 * L) ** 0.25)
    EPS = 1e-5
    SCALE = float(DH) ** -0.5
    KEYS = [P * (t + 1) for t in range(NT)]
    KOFF = [0, P]
    KALL = sum(KEYS)

    A_Q, A_SMALL, B_Q, B_K, B_V, C_Q, C_K, C_V, G_A = 0, 512, 936, 1448, 1960, 2472, 2984, 3496, 4008
    SMALL = B_Q - A_SMALL
    assert WIN == G_A + 3 * D and D == 1024 and NT == 2 and F == 256

    N_ADA = 6 * D // SC
    RING = 3
    items = [("ada", j) for j in range(N_ADA)]
    items += [("qa", 0), ("small", 0), ("qb", 0), ("kb", 0), ("vb", 0), ("qc", 0), ("kc", 0), ("vc", 0)]
    for br in range(3):
        items += [("gate", 2 * br), ("br", br), ("gate", 2 * br + 1)]
    items += [("wout", 0), ("wout", 1), ("ln", 0), ("sh_gu", 0), ("sh_d", 0), ("ln", 1)]
    NI = len(items)
    WAVES = {it: n for n, it in enumerate(items)}
    DMAS_OF = {"sh_gu": 2, "sh_d": 2, "ln": 2}
    WIN_AT = {"qa": A_Q, "small": A_SMALL, "qb": B_Q, "kb": B_K, "vb": B_V, "qc": C_Q, "kc": C_K, "vc": C_V}

    NROPE, NTOK, NIDX, NGB, NJOB = 23, 6, NT * IH, 3 * KD, E + 1

    with ExitStack() as ctx:
        def sb(name, shape, dt=F32):
            return ctx.enter_context(nc.sbuf_tensor(name, shape, dt))

        def sem(name):
            return ctx.enter_context(nc.semaphore(name))

        pb = ctx.enter_context(nc.psum_tensor("pb", [P, 8, 512], F32))

        ring = sb("ring", [P, RING, KD * SC])
        experts = sb("experts", [P, 2, 2, 3, KD * F])
        xs = sb("xs", [P, NT, D])
        uT = sb("uT", [P, KD, S])
        yacc = sb("yacc", [P, NT, D])
        ident = sb("ident", [P, P])
        perm = sb("perm", [P, 2, P])
        rope = sb("rope", [P, 4, S])
        ropei_tok = sb("ropei_tok", [P, 2, NT, ID // 2])
        masks = sb("masks", [P, 3, KALL])
        CAUSAL, DILATED, INDEXED = 0, 1, 2
        ones = sb("ones", [P, P])
        g_bc = sb("g_bc", [P, 2, D])
        modT = sb("modT", [P, 4, KD])
        adaT_bias = sb("adaT_bias", [P, L, 4, KD])
        ikgb = sb("ikgb", [P, L, 2, ID])
        rbias = sb("rbias", [P, L, E])
        silu_c = sb("silu_c", [P, 3, KD])
        acc = sb("acc", [P, 2, SC])
        sg = sb("sg", [P, 2, S])
        small = sb("small", [P, 64])
        stats = sb("stats", [P, 4, 6])
        negmax = sb("negmax", [P, 4, NT])
        esum = sb("esum", [P, 4, NT])
        rden = sb("rden", [P, 4, NT])
        gates = sb("gates", [P, NT, E])
        rt = sb("rt", [P, 5, NT, E])
        top8 = sb("top8", [P, NT, 8, 8])
        hT = sb("hT", [P, 2, KF, S])
        eh = sb("eh", [P, KF * S])
        powc = sb("powc", [P, 2])

        lend = experts[:, 1].rearrange("p e m n -> p (e m n)")
        at = [0]

        def part(*shape):
            n = 1
            for s in shape:
                n *= s
            a = lend[:, at[0]:at[0] + n]
            at[0] += n
            assert at[0] <= 2 * 3 * KD * F
            names = "abc"[:len(shape)]
            if len(shape) == 1:
                return a
            return a.rearrange(f"p ({' '.join(names)}) -> p {' '.join(names)}",
                               **{c: s for c, s in zip(names, shape)})

        qT = [part(4, S) for _ in range(3)]
        kT = [part(1, S), part(4, S), part(4, S)]
        v_a = part(NT, DH)
        v_b = part(NT, 512)
        v_c = part(NT, 512)
        oT = [part(4, S) for _ in range(3)]
        qiT = part(2, S)
        kiT = part(S)
        mergedT = lend[:, 0:KD * S].rearrange("p (k n) -> p k n", k=KD)
        score = hT[:].rearrange("p a k n -> p (a k n)")[:, 0:KALL]
        relu = sg
        ki_tok = rt[:].rearrange("p a t e -> p (a t e)")
        lg = yacc[:].rearrange("p t d -> p (t d)")[:, 0:4 * KALL].rearrange("p (a n) -> p a n", a=4)
        pT = part(2, KALL)
        raw = eh[:].rearrange("p (a n) -> p a n", a=2)
        ropetmp = hT[:].rearrange("p a k n -> p (a k n)")[:, 512:1024].rearrange("p (a n) -> p a n", a=2)

        ki_rows = sb("ki_rows", [P, NT, ID + IH])
        ki_tmp = sb("ki_tmp", [P, NT, ID])
        ki_prod = sb("ki_prod", [P, 4, NT, ID // 2])
        ki_done = sb("ki_done", [P, 1])
        wi = sb("wi", [P, NT, IH])
        mv = sb("mv", [P, NT, 2])
        gscore = sb("gscore", [P, 3, NT, 8])
        gsum = sb("gsum", [P, 2, NT])
        tmp_y = acc

        CONST_LOADS = [
            (xs[:], x.rearrange("(t p) d -> p t d", p=P)), (silu_c[:, 0, :], cT), (ident[:], ident_c), (perm[:], perm_c),
            (rope[:], rope_c), (ropei_tok[:], ropei_tok_c), (masks[:, 0:2, :], mask_c), (adaT_bias[:], adaT_b),
            (ikgb[:].rearrange("p l a i -> p (l a i)"), ik_gb.rearrange("l a i -> (l a i)").partition_broadcast(P)),
            (rbias[:].rearrange("p l e -> p (l e)"), router_bias.rearrange("l e -> (l e)").partition_broadcast(P)),
        ]
        N_CONSTS = len(CONST_LOADS)

        consts_landed = sem("consts_landed")
        ring_landed = [sem(f"ring_landed{i}") for i in range(RING)]
        pair_landed = [sem(f"pair_landed{i}") for i in range(2)]
        gbias_landed = sem("gbias_landed")
        silu_exp = sem("silu_exp")
        silu_den = sem("silu_den")
        ones_ready = sem("ones_ready")
        acc_ready = sem("acc_ready")
        mod_done = sem("mod_done")
        mod_read = sem("mod_read")
        xT_done = sem("xT_done")
        uT_ready = sem("uT_ready")
        proj_done = sem("proj_done")
        raw_ready = sem("raw_ready")
        perm_done = sem("perm_done")
        rope_done = sem("rope_done")
        tok_done = sem("tok_done")
        tok_read = sem("tok_read")
        ki_ready = sem("ki_ready")
        kiT_done = sem("kiT_done")
        kiT_ready = sem("kiT_ready")
        idx_done = sem("idx_done")
        relu_ready = sem("relu_ready")
        score_used = sem("score_used")
        s_done = sem("s_done")
        max_ready = sem("max_ready")
        exp_done = sem("exp_done")
        p_ready = sem("p_ready")
        pt_done = sem("pt_done")
        pt_ready = sem("pt_ready")
        pv_done = sem("pv_done")
        o_read = sem("o_read")
        gb_done = sem("gb_done")
        eg_ready = sem("eg_ready")
        merged_done = sem("merged_done")
        y_done = sem("y_done")
        var_ready = sem("var_ready")
        rstd_ready = sem("rstd_ready")
        norm_done = sem("norm_done")
        router_done = sem("router_done")
        er_ready = sem("er_ready")
        gu_done = sem("gu_done")
        eh_ready = sem("eh_ready")
        h_ready = sem("h_ready")
        down_done = sem("down_done")
        yacc_done = sem("yacc_done")
        dve_chain = sem("dve_chain")
        pool_chain = sem("pool_chain")
        out_stored = sem("out_stored")

        class Chain:

            def __init__(self, eng, s):
                self.eng, self.s, self.n, self.turn = eng, s, 0, 0

            def __call__(self, ins):
                ins.then_inc(self.s, 1)
                self.n += 1
                self.eng.wait_ge(self.s, self.turn + self.n)

        def ring_slot(l, item):
            return (l * NI + WAVES[item]) % RING

        def ring_ap(l, item):
            return ring[:, ring_slot(l, item)]

        def dmas_upto(n_global):
            return sum(DMAS_OF.get(items[n % NI][0], 1) for n in range(n_global % RING, n_global + 1, RING))

        def wait_item(eng, l, item):
            n = l * NI + WAVES[item]
            eng.wait_ge(ring_landed[n % RING], 16 * dmas_upto(n))

        block = ctx.enter_context(nc.Block())

        @block.sync
        def _(sp):
            def used(n):
                l, (kind, j) = n // NI, items[n % NI]
                rope_at = {"qa": 4, "qb": 11, "kb": 15, "qc": 19, "kc": 23}
                tok_at = {"small": 2, "vb": 4, "vc": 6}
                if kind == "ada":
                    sp.wait_ge(acc_ready, N_ADA * l + j + 1)
                elif kind in rope_at:
                    sp.wait_ge(proj_done, NROPE * l + rope_at[kind])
                elif kind in tok_at:
                    sp.wait_ge(tok_done, NTOK * l + tok_at[kind])
                elif kind == "gate":
                    sp.wait_ge(gb_done, NGB * l + 4 * (j + 1))
                elif kind == "br":
                    sp.wait_ge(gb_done, NGB * l + KD * (j + 1))
                elif kind == "wout":
                    sp.wait_ge(y_done, 4 * l + 2 * (j + 1))
                elif kind == "ln":
                    sp.wait_ge(norm_done, 2 * l + j + 1)
                elif kind == "sh_gu":
                    sp.wait_ge(gu_done, NJOB * l + 1)
                else:
                    sp.wait_ge(down_done, NJOB * l + 1)

            def load_item(l, m):
                n = l * NI + m
                kind, j = items[m]
                if n >= RING:
                    used(n - RING)
                dst, s = ring[:, n % RING], ring_landed[n % RING]
                if kind == "ada":
                    sp.dma_start(dst.rearrange("p (k c) -> p k c", k=KD),
                                 ada_w[l, :, j * SC:(j + 1) * SC].rearrange("(p k) c -> p k c", k=KD)).then_inc(s, 16)
                elif kind in WIN_AT or kind == "gate":
                    c0 = WIN_AT[kind] if kind in WIN_AT else G_A + j * SC
                    w = SMALL if kind == "small" else SC
                    sp.dma_start(dst.rearrange("p (k c) -> p k c", k=KD)[:, :, 0:w],
                                 w_in[l, :, c0:c0 + w].rearrange("(p k) c -> p k c", k=KD)).then_inc(s, 16)
                elif kind == "br":
                    w = (w_br_a, w_br_b, w_br_c)[j]
                    sp.dma_start(dst.rearrange("p (b c) -> p b c", b=4),
                                 w[l].rearrange("(b p) c -> p b c", p=P)).then_inc(s, 16)
                elif kind == "wout":
                    sp.dma_start(dst.rearrange("p (k c) -> p k c", k=KD),
                                 w_out[l, :, j * SC:(j + 1) * SC].rearrange("(k p) c -> p k c", p=P)).then_inc(s, 16)
                elif kind == "ln":
                    for m in range(2):
                        sp.dma_start(dst[:, m * D:(m + 1) * D], ln_gb[l, j, m].partition_broadcast(P)).then_inc(s, 16)
                elif kind == "sh_gu":
                    sp.dma_start(dst[:, 0:KD * F], ws_gate[l].rearrange("(p k) c -> p (k c)", k=KD)).then_inc(s, 16)
                    sp.dma_start(dst[:, KD * F:2 * KD * F], ws_up[l].rearrange("(p k) c -> p (k c)", k=KD)).then_inc(s, 16)
                else:
                    sp.dma_start(dst[:, 0:KF * D], ws_down[l].rearrange("(p k) c -> p (k c)", k=KF)).then_inc(s, 16)
                    sp.dma_start(dst[:, KF * D:KF * D + KD * E],
                                 w_router[l].rearrange("(p k) c -> p (k c)", k=KD)).then_inc(s, 16)

            def load_pair(l, slot, e0):
                for m, (w, k) in enumerate(((w_gate, KD), (w_up, KD), (w_down, KF))):
                    sp.dma_start(experts[:, slot, :, m, :],
                                 w[l, bass.ds(e0, 2)].rearrange("e (p k) c -> p e (k c)", k=k)).then_inc(pair_landed[slot], 16)

            for l in range(L):
                for m in range(NI):
                    load_item(l, m)
                    if items[m] == ("vc", 0):
                        if l:
                            sp.wait_ge(down_done, NJOB * l)
                        load_pair(l, 0, 0)
                sp.wait_ge(y_done, 4 * (l + 1))
                load_pair(l, 1, 2)
                with sp.Fori(1, E // 4) as i:
                    for slot in range(2):
                        sp.wait_ge(down_done, i * 4 + (NJOB * l + 1 - 4 + 2 * (slot + 1)))
                        load_pair(l, slot, i * 4 + 2 * slot)
            sp.wait_ge(norm_done, 2 * L)
            sp.dma_start(out.rearrange("(t p) d -> p t d", p=P), xs[:]).then_inc(out_stored, 16)
            sp.wait_ge(out_stored, 16)

        @block.gpsimd
        def _(pool):
            nc.gpsimd.memset(powc[:], -0.5).then_inc(pool_chain, 1)
            pool.wait_ge(pool_chain, 1)

            def rstd(n):
                pool.wait_ge(var_ready, n)
                nc.gpsimd.tensor_tensor(small[:, 4:6], small[:, 2:4], powc[:], ALU.pow).then_inc(rstd_ready, 1)

            for l in range(L):
                if l:
                    pool.wait_ge(norm_done, 2 * l)
                for m, piece in enumerate((2, 5)):
                    pool.dma_start(g_bc[:, m, :], ada_b[l, piece * D:(piece + 1) * D].partition_broadcast(P))\
                        .then_inc(gbias_landed, 16)
                for n in range(3):
                    rstd(3 * l + n + 1)

        @block.tensor
        def _(pe):
            mm = nc.tensor.matmul

            def transpose_x(n):
                for k in range(KD):
                    for t in range(NT):
                        o = (k % 2) * S + t * P
                        ins = nc.tensor.transpose(pb[:, k // 2, o:o + P], xs[:, t, k::KD], ident[:])
                    if k % 2:
                        ins.then_inc(xT_done, 1)

            def contract(dst, lhs, rhs, n):
                for k in range(n):
                    ins = mm(dst, lhs(k), rhs(k), start=(k == 0), stop=(k == n - 1))
                return ins

            def modulation(l):
                for j in range(N_ADA):
                    pe.wait_ge(acc_ready, N_ADA * l + j + 1)
                    if j >= 2:
                        pe.wait_ge(mod_read, N_ADA * l + j - 1)
                    if j // 2 in (2, 5):
                        ins = mm(pb[:, 5 + j % 2, :], ones[:], acc[:, j % 2, :], start=True, stop=True)
                    else:
                        q = (0, 1, None, 2, 3)[j // 2]
                        h = 64 * (j % 2)
                        for k in range(KD):
                            ins = mm(pb[h:h + 64, 7, q * KD + k:q * KD + k + 1], acc[:, j % 2, k::KD], ones[:, 0:1],
                                     start=True, stop=True)
                    ins.then_inc(mod_done, 1)

            def rotate_half(r, l):
                pe.wait_ge(raw_ready, NROPE * l + r + 1)
                if r >= 2:
                    pe.wait_ge(rope_done, NROPE * l + r - 1)
                mm(pb[:, 2 + r % 2, 0:S], perm[:, 1 if r in (5, 6) else 0, :], raw[:, r % 2, :], start=True, stop=True)\
                    .then_inc(perm_done, 1)

            def projections(l):
                r = 0
                for name, blocks in (("qa", 4), ("small", 3), ("qb", 4), ("kb", 4), ("vb", 0), ("qc", 4), ("kc", 4), ("vc", 0)):
                    wait_item(pe, l, (name, 0))
                    w = ring_ap(l, (name, 0)).rearrange("p (k c) -> p k c", k=KD)
                    for b in range(blocks):
                        if r >= 2:
                            pe.wait_ge(raw_ready, NROPE * l + r - 1)
                        if name == "small" and b == 0:
                            for h in range(2):
                                ins = contract(pb[64 * h:64 * h + 64, r % 2, 0:S], lambda k: w[:, k, 0:DH],
                                               lambda k: uT[:, k, :], KD)
                        else:
                            c0 = b * P if name != "small" else 2 * DH + (b - 1) * P
                            ins = contract(pb[:, r % 2, 0:S], lambda k: w[:, k, c0:c0 + P], lambda k: uT[:, k, :], KD)
                        ins.then_inc(proj_done, 1)
                        if r:
                            rotate_half(r - 1, l)
                        r += 1
                    if name in ("small", "vb", "vc"):
                        g = ("small", "vb", "vc").index(name)
                        for t in range(NT):
                            if g:
                                pe.wait_ge(tok_read, NTOK * l + 2 * (g - 1) + t + 1)
                            lhs = lambda k: uT[:, k, t * P:(t + 1) * P]
                            if g == 0:
                                contract(pb[:, 4 + t, 0:DH], lhs, lambda k: w[:, k, DH:2 * DH], KD)
                                ins = contract(pb[:, 4 + t, DH:DH + ID + IH], lhs, lambda k: w[:, k, 384:384 + ID + IH], KD)
                            else:
                                ins = contract(pb[:, 4 + t, :], lhs, lambda k: w[:, k, :], KD)
                            ins.then_inc(tok_done, 1)
                rotate_half(r - 1, l)

            def indexer(l):
                pe.wait_ge(ki_ready, l + 1)
                for t in range(NT):
                    ins = nc.tensor.transpose(pb[:, 6, t * P:(t + 1) * P], ki_tok[:, t * P:(t + 1) * P], ident[:])
                ins.then_inc(kiT_done, 1)
                pe.wait_ge(kiT_ready, l + 1)
                pe.wait_ge(rope_done, NROPE * (l + 1))
                pe.wait_ge(tok_read, NTOK * (l + 1))
                i = 0
                for t in range(NT):
                    for h in range(IH):
                        if i >= 2:
                            pe.wait_ge(relu_ready, NIDX * l + i - 1)
                        r = ID * (h % 4)
                        mm(pb[:, 4 + i % 2, 0:KEYS[t]], qiT[r:r + ID, h // 4, t * P:(t + 1) * P], kiT[r:r + ID, 0:KEYS[t]],
                           start=True, stop=True, tile_position=(r, 0)).then_inc(idx_done, 1)
                        i += 1

            ORDER = [(br, h) for br in (1, 2, 0) for h in range(8)]

            def scores(l, i):
                br, h = ORDER[i]
                r = DH * (h % 2)
                if i >= 2:
                    pe.wait_ge(max_ready, HC * l + i - 1)
                for t in range(NT):
                    ins = mm(pb[:, i % 2, KOFF[t]:KOFF[t] + KEYS[t]], qT[br][r:r + DH, h // 2, t * P:(t + 1) * P],
                             kT[br][r:r + DH, (h // 2 if br else 0), 0:KEYS[t]], start=True, stop=True)
                ins.then_inc(s_done, 1)

            def turn_probs(l, i):
                pe.wait_ge(p_ready, HC * l + i + 1)
                if i >= 2:
                    pe.wait_ge(pt_ready, HC * l + i - 1)
                for m in range(3):
                    ins = nc.tensor.transpose(pb[:, 2 + i % 2, m * P:(m + 1) * P], lg[:, i % 4, m * P:(m + 1) * P], ident[:])
                ins.then_inc(pt_done, 1)

            def values(l, i):
                br, h = ORDER[i]
                hp = i // 2
                pe.wait_ge(pt_ready, HC * l + i + 1)
                if i % 2 == 0 and hp >= 2:
                    pe.wait_ge(o_read, HC // 2 * l + hp - 1)
                v = (v_a, v_b, v_c)[br]
                c = 0 if br == 0 else h * DH
                o = pb[DH * (h % 2):DH * (h % 2) + DH, 4 + hp % 2, 0:S]
                mm(o, v[:, 0, c:c + DH], pT[:, i % 2, 0:S], start=True, stop=False)
                mm(o[:, P:S], v[:, 1, c:c + DH], pT[:, i % 2, S:S + P], start=False, stop=True).then_inc(pv_done, 1)

            def attention(l):
                for i in range(HC + 3):
                    if i < HC:
                        scores(l, i)
                    if 2 <= i < HC + 2:
                        turn_probs(l, i - 2)
                    if 3 <= i:
                        values(l, i - 3)

            def branches(l):
                pe.wait_ge(o_read, HC // 2 * (l + 1))
                for br in range(3):
                    wait_item(pe, l, ("br", br))
                    wb = ring_ap(l, ("br", br)).rearrange("p (b c) -> p b c", b=4)
                    for k in range(KD):
                        j = br * KD + k
                        if k % 4 == 0:
                            wait_item(pe, l, ("gate", 2 * br + k // 4))
                        wg = ring_ap(l, ("gate", 2 * br + k // 4)).rearrange("p (k c) -> p k c", k=KD)
                        if j >= 2:
                            pe.wait_ge(merged_done, NGB * l + j - 1)
                        contract(pb[:, 2 + j % 2, 0:S], lambda b: wb[:, b, k * P:(k + 1) * P], lambda b: oT[br][:, b, :], 4)
                        contract(pb[:, j % 2, 0:S], lambda q: wg[:, q, (k % 4) * P:(k % 4 + 1) * P],
                                 lambda q: uT[:, q, :], KD).then_inc(gb_done, 1)

            def mix_out(l):
                pe.wait_ge(merged_done, NGB * (l + 1))
                for half in range(2):
                    wait_item(pe, l, ("wout", half))
                    w = ring_ap(l, ("wout", half)).rearrange("p (k c) -> p k c", k=KD)
                    for t in range(NT):
                        contract(pb[:, 4 + 2 * half + t, :], lambda k: mergedT[:, k, t * P:(t + 1) * P],
                                 lambda k: w[:, k, :], KD).then_inc(y_done, 1)

            def router(l):
                wait_item(pe, l, ("sh_d", 0))
                w = ring_ap(l, ("sh_d", 0))[:, KF * D:KF * D + KD * E].rearrange("p (k c) -> p k c", k=KD)
                pe.wait_ge(uT_ready, 2 * KD * (l + 1))
                for t in range(NT):
                    ins = contract(pb[:, 2, t * E:(t + 1) * E], lambda k: uT[:, k, t * P:(t + 1) * P], lambda k: w[:, k, :], KD)
                ins.then_inc(router_done, 1)
                pe.wait_ge(er_ready, l + 1)

            def gate_up(bank, wg, wu, reuse):
                if reuse is not None:
                    pe.wait_ge(h_ready, reuse)
                for q, w in enumerate((wg, wu)):
                    for m in range(KF):
                        ins = contract(pb[:, bank + q, m * S:(m + 1) * S], lambda k: w[:, k, m::KF], lambda k: uT[:, k, :], KD)
                ins.then_inc(gu_done, 1)

            def down(n, hs, wd):
                pe.wait_ge(h_ready, n)
                for t in range(NT):
                    for half in range(2):
                        ins = contract(pb[:, 4 + 2 * half + t, :], lambda k: hT[:, hs, k, t * P:(t + 1) * P],
                                       lambda k: wd[:, k, half * 512:(half + 1) * 512], KF)
                ins.then_inc(down_done, 1)

            def expert_parts(slot, e):
                return (experts[:, slot, e, 0, :].rearrange("p (k c) -> p k c", k=KD),
                        experts[:, slot, e, 1, :].rearrange("p (k c) -> p k c", k=KD),
                        experts[:, slot, e, 2, :].rearrange("p (k c) -> p k c", k=KF))

            for l in range(L):
                pe.wait_ge(consts_landed, 16 * N_CONSTS)
                pe.wait_ge(ones_ready, 1)
                if l:
                    pe.wait_ge(norm_done, 2 * l)
                modulation(l)
                transpose_x(2 * l)
                pe.wait_ge(uT_ready, KD * (2 * l + 1))
                pe.wait_ge(mod_read, N_ADA * (l + 1))
                projections(l)
                indexer(l)
                attention(l)
                branches(l)
                mix_out(l)
                pe.wait_ge(norm_done, 2 * l + 1)
                transpose_x(2 * l + 1)
                router(l)
                J = NJOB * l
                wait_item(pe, l, ("sh_gu", 0))
                w = ring_ap(l, ("sh_gu", 0))
                gate_up(0, w[:, 0:KD * F].rearrange("p (k c) -> p k c", k=KD),
                        w[:, KD * F:2 * KD * F].rearrange("p (k c) -> p k c", k=KD), None)
                down(J + 1, 0, ring_ap(l, ("sh_d", 0))[:, 0:KF * D].rearrange("p (k c) -> p k c", k=KF))
                with pe.Fori(0, E // 4) as i:
                    for e in range(4):
                        wg, wu, wd = expert_parts(e // 2, e % 2)
                        if e % 2 == 0:
                            pe.wait_ge(pair_landed[e // 2], i * 48 + (48 * (E // 4) * l + 48))
                        gate_up(2 * (e % 2), wg, wu, i * 4 + (J + e))
                        if e:
                            pe.wait_ge(yacc_done, i * 4 + (J + e))
                            down(i * 4 + (J + e + 1), e % 2, expert_parts((e - 1) // 2, (e - 1) % 2)[2])
                    pe.wait_ge(yacc_done, i * 4 + (J + 4))
                    down(i * 4 + (J + 5), 0, expert_parts(1, 1)[2])

        @block.scalar
        def _(act):
            def cp(dst, src):
                return nc.scalar.copy(dst, src)

            for dst, src in CONST_LOADS:
                act.dma_start(dst, src).then_inc(consts_landed, 16)
            act.wait_ge(consts_landed, 16 * N_CONSTS)
            nc.scalar.activation(silu_c[:, 1, :], silu_c[:, 0, :], ACT.Exp, scale=-1.0).then_inc(silu_exp, 1)

            def rotary(l, r):
                act.wait_ge(proj_done, NROPE * l + r + 1)
                if r >= 2:
                    act.wait_ge(rope_done, NROPE * l + r - 1)
                cp(raw[:, r % 2, :], pb[:, r % 2, 0:S]).then_inc(raw_ready, 1)

            def token_rows(l, g):
                for t in range(NT):
                    act.wait_ge(tok_done, NTOK * l + 2 * g + t + 1)
                    if g == 0:
                        cp(v_a[:, t, :], pb[:, 4 + t, 0:DH])
                        cp(ki_rows[:, t, :], pb[:, 4 + t, DH:DH + ID + IH]).then_inc(tok_read, 1)
                    else:
                        cp((v_b, v_c)[g - 1][:, t, :], pb[:, 4 + t, :]).then_inc(tok_read, 1)

            def soft(l, i):
                act.wait_ge(max_ready, HC * l + i + 1)
                for t in range(NT):
                    a = lg[:, i % 4, KOFF[t]:KOFF[t] + KEYS[t]]
                    ins = nc.scalar.activation(a, a, ACT.Exp, bias=negmax[:, i % 4, t:t + 1],
                                               accum_out=esum[:, i % 4, t:t + 1])
                ins.then_inc(exp_done, 1)

            def probs_out(l, i):
                act.wait_ge(pt_done, HC * l + i + 1)
                if i >= 2:
                    act.wait_ge(pv_done, HC * l + i - 1)
                cp(pT[:, i % 2, :], pb[:, 2 + i % 2, 0:KALL]).then_inc(pt_ready, 1)

            def heads_out(l, hp):
                act.wait_ge(pv_done, HC * l + 2 * hp + 2)
                br = (1, 2, 0)[hp // 4]
                cp(oT[br][:, hp % 4, :], pb[:, 4 + hp % 2, 0:S]).then_inc(o_read, 1)

            def ffn_exp(n, bank):
                act.wait_ge(gu_done, n)
                nc.scalar.activation(eh[:], pb[:, bank, :], ACT.Exp, scale=-1.0).then_inc(eh_ready, 1)

            for l in range(L):
                r = 0
                for blocks, tok in ((7, 0), (8, 1), (8, 2)):
                    for _ in range(blocks):
                        rotary(l, r)
                        r += 1
                    token_rows(l, tok)
                act.wait_ge(kiT_done, l + 1)
                cp(kiT, pb[:, 6, 0:S]).then_inc(kiT_ready, 1)
                i = 0
                for t in range(NT):
                    for h in range(IH):
                        act.wait_ge(idx_done, NIDX * l + i + 1)
                        if i >= 2:
                            act.wait_ge(score_used, NIDX * l + i - 1)
                        nc.scalar.activation(relu[:, i % 2, 0:KEYS[t]], pb[:, 4 + i % 2, 0:KEYS[t]], ACT.Relu,
                                             scale=float(ID) ** -0.5).then_inc(relu_ready, 1)
                        i += 1
                for i in range(HC + 3):
                    if i < HC:
                        soft(l, i)
                    if 2 <= i < HC + 2:
                        probs_out(l, i - 2)
                    if i >= 4 and i % 2 == 0:
                        heads_out(l, (i - 4) // 2)
                for j in range(NGB):
                    act.wait_ge(gb_done, NGB * l + j + 1)
                    if j >= 2:
                        act.wait_ge(merged_done, NGB * l + j - 1)
                    nc.scalar.activation(sg[:, j % 2, :], pb[:, j % 2, 0:S], ACT.Exp, scale=-1.0).then_inc(eg_ready, 1)
                act.wait_ge(router_done, l + 1)
                nc.scalar.activation(rt[:, 0, :, :], pb[:, 2, 0:NT * E].rearrange("p (t e) -> p t e", t=NT), ACT.Exp,
                                     scale=-1.0).then_inc(er_ready, 1)
                ffn_exp(NJOB * l + 1, 0)
                with act.Fori(0, E // 4) as i:
                    for e in range(4):
                        act.wait_ge(h_ready, i * 4 + (NJOB * l + e + 1))
                        ffn_exp(i * 4 + (NJOB * l + e + 2), 2 * (e % 2))

        @block.vector
        def _(dve):
            v = nc.vector
            link = Chain(dve, dve_chain)
            v.memset(ones[:], 1.0).then_inc(ones_ready, 1)
            dve.wait_ge(consts_landed, 16 * N_CONSTS)
            dve.wait_ge(silu_exp, 1)
            link(v.tensor_scalar(silu_c[:, 1, :], silu_c[:, 1, :], 1.0, None, ALU.add))
            link(v.reciprocal(silu_c[:, 2, :], silu_c[:, 1, :]))
            link(v.tensor_tensor(silu_c[:, 1, :], silu_c[:, 0, :], silu_c[:, 2, :], ALU.mult))

            def mod_evacuate(l, j):
                dve.wait_ge(mod_done, N_ADA * l + j + 1)
                piece, half = j // 2, j % 2
                if piece in (2, 5):
                    q = (piece - 2) // 3
                    if piece == 2 and half == 0:
                        dve.wait_ge(gbias_landed, 32 * (l + 1))
                    a = g_bc[:, q, half * SC:(half + 1) * SC]
                    v.scalar_tensor_tensor(a, pb[:, 5 + half, :], 1.0, a, ALU.add, ALU.add).then_inc(mod_read, 1)
                else:
                    q = (0, 1, None, 2, 3)[piece]
                    h = slice(64 * half, 64 * half + 64)
                    v.scalar_tensor_tensor(modT[h, q, :], pb[h, 7, q * KD:(q + 1) * KD], float(q % 2),
                                           adaT_bias[h, l, q, :], ALU.add, ALU.add).then_inc(mod_read, 1)

            def modulation(l):
                for j in range(N_ADA):
                    wait_item(dve, l, ("ada", j))
                    w = ring_ap(l, ("ada", j)).rearrange("p (k c) -> p k c", k=KD)
                    if j >= 2:
                        dve.wait_ge(mod_done, N_ADA * l + j - 1)
                    a = acc[:, j % 2, :]
                    link(v.tensor_scalar(a, w[:, 0, :], silu_c[:, 1, 0:1], None, ALU.mult))
                    for k in range(1, KD):
                        ins = v.scalar_tensor_tensor(a, w[:, k, :], silu_c[:, 1, k:k + 1], a, ALU.mult, ALU.add)
                        if k < KD - 1:
                            link(ins)
                    ins.then_inc(acc_ready, 1)
                    if j:
                        mod_evacuate(l, j - 1)
                mod_evacuate(l, N_ADA - 1)
                dve.wait_ge(mod_read, N_ADA * (l + 1))

            def modulate(n):
                for k in range(KD):
                    dve.wait_ge(xT_done, KD // 2 * n + k // 2 + 1)
                    q = 2 * (n % 2)
                    v.tensor_scalar(uT[:, k, :], pb[:, k // 2, (k % 2) * S:(k % 2 + 1) * S], modT[:, q + 1, k:k + 1],
                                    modT[:, q, k:k + 1], ALU.mult, ALU.add).then_inc(uT_ready, 1)

            ROPE_DST = [qT[0][:, b, :] for b in range(4)] + [kT[0][:, 0, :]] + [qiT[:, b, :] for b in range(2)]
            for br in (1, 2):
                ROPE_DST += [qT[br][:, b, :] for b in range(4)] + [kT[br][:, b, :] for b in range(4)]

            def rotary(l, r):
                q = 2 if r in (5, 6) else 0
                dve.wait_ge(raw_ready, NROPE * l + r + 1)
                if r:
                    dve.wait_ge(rope_done, NROPE * l + r)
                v.tensor_tensor(ropetmp[:, 0, :], raw[:, r % 2, :], rope[:, q, :], ALU.mult)
                dve.wait_ge(perm_done, NROPE * l + r + 1)
                link(v.tensor_tensor(ropetmp[:, 1, :], pb[:, 2 + r % 2, 0:S], rope[:, q + 1, :], ALU.mult))
                v.tensor_tensor(ROPE_DST[r], ropetmp[:, 0, :], ropetmp[:, 1, :], ALU.add).then_inc(rope_done, 1)

            def indexer_keys(l):
                dve.wait_ge(tok_read, NTOK * l + 2)
                for t in range(NT):
                    ins = v.bn_stats(stats[:, t, :], ki_rows[:, t, 0:ID])
                link(ins)
                for t in range(NT):
                    ins = v.bn_aggr(mv[:, t, :], stats[:, t, :])
                link(ins)
                v.tensor_scalar(small[:, 2:4], mv[:, :, 1], EPS, None, ALU.add).then_inc(var_ready, 1)
                dve.wait_ge(rstd_ready, 3 * l + 1)
                kn = ki_tmp
                for t in range(NT):
                    ins = v.tensor_scalar(kn[:, t, :], ki_rows[:, t, 0:ID], mv[:, t, 0:1], small[:, 4 + t:5 + t],
                                          ALU.subtract, ALU.mult)
                link(ins)
                for t in range(NT):
                    ins = v.tensor_tensor(kn[:, t, :], kn[:, t, :], ikgb[:, l, 0, :], ALU.mult)
                link(ins)
                for t in range(NT):
                    ins = v.tensor_tensor(kn[:, t, :], kn[:, t, :], ikgb[:, l, 1, :], ALU.add)
                link(ins)
                H = ID // 2
                x1, x2 = kn[:, :, 0:H], kn[:, :, H:ID]
                v.tensor_tensor(ki_prod[:, 0], x1, ropei_tok[:, 0], ALU.mult)
                v.tensor_tensor(ki_prod[:, 1], x2, ropei_tok[:, 1], ALU.mult)
                v.tensor_tensor(ki_prod[:, 2], x2, ropei_tok[:, 0], ALU.mult)
                link(v.tensor_tensor(ki_prod[:, 3], x1, ropei_tok[:, 1], ALU.mult))
                dst = ki_tok[:, 0:NT * P].rearrange("p (t c i) -> p t c i", t=NT, c=4)
                for c in range(4):
                    v.tensor_tensor(dst[:, :, c, 0:H], ki_prod[:, 0], ki_prod[:, 1], ALU.subtract)
                    ins = v.tensor_tensor(dst[:, :, c, H:ID], ki_prod[:, 2], ki_prod[:, 3], ALU.add)
                link(v.tensor_scalar(wi[:], ki_rows[:, :, ID:ID + IH], float(IH) ** -0.5, None, ALU.mult))
                ins = v.tensor_copy(ki_done[:], wi[:, 0, 0:1])
                ins.then_inc(ki_ready, 1)

            def indexer(l):
                i = 0
                for t in range(NT):
                    o = slice(KOFF[t], KOFF[t] + KEYS[t])
                    for h in range(IH):
                        dve.wait_ge(relu_ready, NIDX * l + i + 1)
                        other = masks[:, CAUSAL, o] if h == 0 else score[:, o]
                        v.scalar_tensor_tensor(score[:, o], relu[:, i % 2, 0:KEYS[t]], wi[:, t, h:h + 1], other,
                                               ALU.mult, ALU.add).then_inc(score_used, 1)
                        i += 1
                        dve.wait_ge(score_used, NIDX * l + i)
                for n in range(TOPK_ROUNDS):
                    for t in range(NT):
                        o = slice(KOFF[t], KOFF[t] + KEYS[t])
                        ins = v.max(top8[:, t, n, :], score[:, o])
                    link(ins)
                    for t in range(NT):
                        o = slice(KOFF[t], KOFF[t] + KEYS[t])
                        ins = v.match_replace(score[:, o], top8[:, t, n, :], score[:, o], NEG)
                    link(ins)
                link(v.tensor_scalar(masks[:, INDEXED, :], score, SELECTED, NEG, ALU.is_ge, ALU.mult))
                link(v.tensor_tensor(masks[:, INDEXED, :], masks[:, INDEXED, :], masks[:, CAUSAL, :], ALU.add))

            MASK_OF = (DILATED, CAUSAL, INDEXED)

            def logits(l, i):
                dve.wait_ge(s_done, HC * l + i + 1)
                if i >= 4:
                    dve.wait_ge(pt_done, HC * l + i - 3)
                link(v.scalar_tensor_tensor(lg[:, i % 4, :], pb[:, i % 2, 0:KALL], SCALE, masks[:, MASK_OF[i // 8], :],
                                            ALU.mult, ALU.add))
                for t in range(NT):
                    ins = v.tensor_reduce(negmax[:, i % 4, t:t + 1], lg[:, i % 4, KOFF[t]:KOFF[t] + KEYS[t]], AX.X, ALU.max,
                                          negate=True)
                ins.then_inc(max_ready, 1)

            def normalise(l, i):
                dve.wait_ge(exp_done, HC * l + i + 1)
                link(v.reciprocal(rden[:, i % 4, :], esum[:, i % 4, :]))
                for t in range(NT):
                    a = lg[:, i % 4, KOFF[t]:KOFF[t] + KEYS[t]]
                    ins = v.tensor_scalar(a, a, rden[:, i % 4, t:t + 1], None, ALU.mult)
                ins.then_inc(p_ready, 1)

            def sigmoid_den(a):
                link(v.tensor_scalar(a, a, 1.0, None, ALU.add))
                link(v.reciprocal(a, a))

            def merge(l):
                for j in range(NGB):
                    dve.wait_ge(eg_ready, NGB * l + j + 1)
                    a = sg[:, j % 2, :]
                    sigmoid_den(a)
                    m = mergedT[:, j % KD, :]
                    if j < KD:
                        v.tensor_tensor(m, a, pb[:, 2 + j % 2, 0:S], ALU.mult).then_inc(merged_done, 1)
                    else:
                        link(v.tensor_tensor(a, a, pb[:, 2 + j % 2, 0:S], ALU.mult))
                        v.tensor_tensor(m, m, a, ALU.add).then_inc(merged_done, 1)
                dve.wait_ge(merged_done, NGB * (l + 1))

            def norm(n, parts):
                for (t, half), y in parts:
                    o = slice(half * 512, half * 512 + 512)
                    yield_to = tmp_y[:, (2 * half + t) % 2, :]
                    link(v.tensor_tensor(yield_to, y, g_bc[:, n % 2, o], ALU.mult))
                    link(v.scalar_tensor_tensor(xs[:, t, o], xs[:, t, o], ALPHA, yield_to, ALU.mult, ALU.add))
                    link(v.bn_stats(stats[:, 2 * t + half, :], xs[:, t, o]))
                for t in range(NT):
                    ins = v.bn_aggr(mv[:, t, :], stats[:, 2 * t:2 * t + 2, :])
                link(ins)
                v.tensor_scalar(small[:, 2:4], mv[:, :, 1], EPS, None, ALU.add).then_inc(var_ready, 1)
                dve.wait_ge(rstd_ready, 3 * (n // 2) + 2 + n % 2)
                wait_item(dve, n // 2, ("ln", n % 2))
                ln_bc = ring_ap(n // 2, ("ln", n % 2))[:, 0:2 * D].rearrange("p (m d) -> p m d", m=2)
                for t in range(NT):
                    link(v.tensor_scalar(xs[:, t, :], xs[:, t, :], mv[:, t, 0:1], small[:, 4 + t:5 + t], ALU.subtract, ALU.mult))
                    link(v.tensor_tensor(xs[:, t, :], xs[:, t, :], ln_bc[:, 0, :], ALU.mult))
                    ins = v.tensor_tensor(xs[:, t, :], xs[:, t, :], ln_bc[:, 1, :], ALU.add)
                    if t < NT - 1:
                        link(ins)
                ins.then_inc(norm_done, 1)

            def route(l):
                dve.wait_ge(er_ready, l + 1)
                sc, biased, gm, w = rt[:, 0], rt[:, 1], rt[:, 2], rt[:, 3]
                sigmoid_den(sc)
                for t in range(NT):
                    ins = v.tensor_tensor(biased[:, t, :], sc[:, t, :], rbias[:, l, :], ALU.add)
                link(ins)
                G = 8
                for t in range(NT):
                    for g in range(G):
                        ins = v.max(top8[:, t, g, :], biased[:, t, g * G:(g + 1) * G])
                link(ins)
                gs = gscore
                link(v.tensor_tensor(gs[:, 0], top8[:, :, :, 0], top8[:, :, :, 1], ALU.add))
                for t in range(NT):
                    ins = v.max(gs[:, 1, t, :], gs[:, 0, t, :])
                link(ins)
                link(v.memset(gs[:, 1, :, 4:8], -NEG))
                for t in range(NT):
                    ins = v.match_replace(gs[:, 2, t, :], gs[:, 1, t, :], gs[:, 0, t, :], NEG)
                link(ins)
                link(v.tensor_scalar(gs[:, 2], gs[:, 2], SELECTED, NEG, ALU.is_ge, ALU.mult))
                for g in range(G):
                    for t in range(NT):
                        ins = v.tensor_scalar(gm[:, t, g * G:(g + 1) * G], biased[:, t, g * G:(g + 1) * G],
                                              gs[:, 2, t, g:g + 1], None, ALU.add)
                link(ins)
                for t in range(NT):
                    ins = v.max(top8[:, t, 0, :], gm[:, t, :])
                link(ins)
                for t in range(NT):
                    ins = v.match_replace(w[:, t, :], top8[:, t, 0, :], gm[:, t, :], 2 * NEG)
                link(ins)
                link(v.tensor_scalar(w, w, 1.5 * NEG, None, ALU.is_lt))
                link(v.tensor_tensor(w, w, sc, ALU.mult))
                link(v.tensor_reduce(gsum[:, 0, :], w, AX.X, ALU.add))
                link(v.reciprocal(gsum[:, 1, :], gsum[:, 0, :]))
                for t in range(NT):
                    ins = v.tensor_scalar(gates[:, t, :], w[:, t, :], gsum[:, 1, t:t + 1], 2.5, ALU.mult, ALU.mult)
                link(ins)

            def ffn_h(n, bank, hs):
                dve.wait_ge(eh_ready, n)
                a = eh[:]
                sigmoid_den(a)
                link(v.tensor_tensor(a, a, pb[:, bank, :], ALU.mult))
                v.tensor_tensor(hT[:, hs].rearrange("p k n -> p (k n)"), a, pb[:, bank + 1, :], ALU.mult).then_inc(h_ready, 1)

            def add_y(n, gate):
                dve.wait_ge(down_done, n)
                for t in range(NT):
                    for half in range(2):
                        a = yacc[:, t, half * 512:(half + 1) * 512]
                        y = pb[:, 4 + 2 * half + t, :]
                        if gate is None:
                            ins = v.tensor_copy(a, y)
                        else:
                            ins = v.scalar_tensor_tensor(a, y, gate(t), a, ALU.mult, ALU.add)
                ins.then_inc(yacc_done, 1)

            for l in range(L):
                J = NJOB * l
                modulation(l)
                modulate(2 * l)
                for r in range(7):
                    rotary(l, r)
                indexer_keys(l)
                for r in range(7, NROPE):
                    rotary(l, r)
                indexer(l)
                for i in range(HC + 1):
                    if i < HC:
                        logits(l, i)
                    if i:
                        normalise(l, i - 1)
                merge(l)
                dve.wait_ge(y_done, 4 * (l + 1))
                norm(2 * l, [((t, half), pb[:, 4 + 2 * half + t, :]) for half in range(2) for t in range(NT)])
                modulate(2 * l + 1)
                route(l)
                ffn_h(J + 1, 0, 0)
                add_y(J + 1, None)
                K = 4 * 3
                turn0, n0 = link.turn, link.n
                with dve.Fori(0, E // 4) as i:
                    link.turn = i * K
                    flat = gates[:].rearrange("p t e -> p (t e)")
                    for e in range(4):
                        ffn_h(i * 4 + (J + e + 2), 2 * (e % 2), (e + 1) % 2)
                        if e:
                            add_y(i * 4 + (J + e + 1), lambda t: flat[:, bass.ds(i * 4 + (t * E + e - 1), 1)])
                            dve.wait_ge(yacc_done, i * 4 + (J + e + 1))
                    add_y(i * 4 + (J + 5), lambda t: flat[:, bass.ds(i * 4 + (t * E + 3), 1)])
                    dve.wait_ge(yacc_done, i * 4 + (J + 5))
                assert link.n - n0 == K
                link.turn, link.n = turn0, n0 + K * (E // 4)
                norm(2 * l + 1, [((t, half), yacc[:, t, half * 512:(half + 1) * 512]) for half in range(2) for t in range(NT)])


def constants(S):
    import numpy as np
    P, NEG = 128, np.float32(-1.0e30)
    NT = S // P

    def rope_tables(dim):
        inv = np.float32(10000.0) ** (-np.arange(0, dim, 2, dtype=np.float32) / np.float32(dim))
        ang = np.arange(S, dtype=np.float32)[:, None] * inv[None, :].astype(np.float32)
        return np.cos(ang, dtype=np.float32), np.sin(ang, dtype=np.float32)

    rope = np.zeros((P, 4, S), np.float32)
    perm = np.zeros((P, 2, P), np.float32)
    for n, dim in enumerate((64, 32)):
        c, s = rope_tables(dim)
        h = dim // 2
        for p in range(P):
            rope[p, 2 * n], rope[p, 2 * n + 1] = c[:, p % h], s[:, p % h]
            if p % dim < h:
                perm[p + h, n, p] = -1.0
            else:
                perm[p - h, n, p] = 1.0
    c, s = rope_tables(32)
    ropei = np.stack([c.reshape(NT, P, 16), s.reshape(NT, P, 16)]).transpose(2, 0, 1, 3)
    masks = np.full((P, 2, P + S), NEG, np.float32)
    for t, off in ((0, 0), (1, P)):
        q = (t * P + np.arange(P))[:, None]
        k = np.arange(P * (t + 1))[None, :]
        d = q - k
        masks[:, 0, off:off + P * (t + 1)] = np.where(d >= 0, np.float32(0), NEG)
        count = np.zeros(d.shape, np.int64)
        for window, dil in ((128, 1), (512, 4), (2048, 16)):
            count += (d >= 0) & (d <= window) & (d % dil == 0)
        masks[:, 1, off:off + P * (t + 1)] = np.where(count > 0, np.log(np.maximum(count, 1)), NEG)
    return {"ident": np.eye(P, dtype=np.float32), "perm": perm, "rope": rope,
            "ropei_tok": np.ascontiguousarray(ropei), "masks": masks}


def kernel(**inputs):
    import numpy as _np
    import concourse.bacc as _bacc
    from concourse import mybir as _mybir
    from concourse.bass_utils import run_bass_kernel_spmd as _run

    g = {n: _np.asarray(a) for n, a in inputs.items()}
    L, D, KD = g["w_in"].shape[0], g["w_in"].shape[1], 8
    c = constants(g["x"].shape[1])
    ada_b = g["ada_b"].reshape(L, 6, 128, KD)
    arrays = {
        "x": g["x"][0], "cT": g["c"].reshape(128, KD), "ada_w": g["ada_w"],
        "adaT_b": _np.ascontiguousarray(ada_b[:, (0, 1, 3, 4)].transpose(2, 0, 1, 3)), "ada_b": g["ada_b"],
        "w_in": g["w_in"], "ik_gb": _np.stack([g["ik_norm_g"], g["ik_norm_b"]], 1),
        "w_br_a": g["w_br_a"], "w_br_b": g["w_br_b"], "w_br_c": g["w_br_c"], "w_out": g["w_out"],
        "ln_gb": _np.stack([_np.stack([g["ln1_g"], g["ln1_b"]], 1), _np.stack([g["ln2_g"], g["ln2_b"]], 1)], 1),
        "w_router": g["w_router"], "router_bias": g["router_bias"],
        "w_gate": g["w_gate"], "w_up": g["w_up"], "w_down": g["w_down"],
        "ws_gate": g["ws_gate"], "ws_up": g["ws_up"], "ws_down": g["ws_down"],
        "ident_c": c["ident"], "perm_c": c["perm"], "rope_c": c["rope"], "ropei_tok_c": c["ropei_tok"], "mask_c": c["masks"],
    }
    nc = _bacc.Bacc("TRN2", target_bir_lowering=False, num_devices=1)
    given, args = {}, []
    for name, a in arrays.items():
        a = _np.ascontiguousarray(a)
        given[f"in_{name}"] = a
        args.append(nc.dram_tensor(f"in_{name}", a.shape, _mybir.dt.from_np(a.dtype), kind="ExternalInput").ap())
    args.append(nc.dram_tensor("out_0", g["x"].shape[1:], F32, kind="ExternalOutput").ap())
    build(nc, *args)
    r = _run(nc, [given], core_ids=[0])
    return r.results[0]["out_0"][None]
```

```python
from contextlib import ExitStack

import concourse.bass as bass
from concourse import mybir

F32 = mybir.dt.float32
ALU = mybir.AluOpType
ACT = mybir.ActivationFunctionType
AX = mybir.AxisListType

P = 128
NEG = -1.0e30
SELECTED = -5.0e29
LIMIT = 64


def build(nc, x, cT, ada_w, adaT_b, ada_b, w_in, ik_gb, w_br_a, w_br_b, w_br_c, w_out, ln_gb,
          w_router, router_bias, w_gate, w_up, w_down, ws_gate, ws_up, ws_down,
          ident_c, perm_c, rope_c, ropei_tok_c, mask_c, before_c, slot_c, out):
    L, D, WIN = w_in.shape
    S = x.shape[0]
    E, F = w_gate.shape[1], w_gate.shape[3]
    DH, IH, ID = 64, 8, 32
    KD = D // P
    KF = F // P
    NT = S // P
    SC = 512
    HC = 3 * 8
    TOPK_ROUNDS = 64 // 8
    ALPHA = float((2 * L) ** 0.25)
    EPS = 1e-5
    SCALE = float(DH) ** -0.5
    KEYS = [P * (t + 1) for t in range(NT)]
    KOFF = [0, P]
    KALL = sum(KEYS)

    A_Q, A_SMALL, B_Q, B_K, B_V, C_Q, C_K, C_V, G_A = 0, 512, 936, 1448, 1960, 2472, 2984, 3496, 4008
    SMALL = B_Q - A_SMALL
    assert WIN == G_A + 3 * D and D == 1024 and NT == 2 and F == 256

    N_ADA = 6 * D // SC
    RING = 3
    items = [("ada", j) for j in range(N_ADA)]
    items += [("qa", 0), ("small", 0), ("qb", 0), ("kb", 0), ("vb", 0), ("qc", 0), ("kc", 0), ("vc", 0)]
    for br in range(3):
        items += [("gate", 2 * br), ("br", br), ("gate", 2 * br + 1)]
    items += [("wout", 0), ("wout", 1), ("ln", 0), ("sh_gu", 0), ("sh_d", 0), ("ln", 1)]
    NI = len(items)
    WAVES = {it: n for n, it in enumerate(items)}
    DMAS_OF = {"sh_gu": 2, "sh_d": 2, "ln": 2}
    WIN_AT = {"qa": A_Q, "small": A_SMALL, "qb": B_Q, "kb": B_K, "vb": B_V, "qc": C_Q, "kc": C_K, "vc": C_V}

    NROPE, NTOK, NIDX, NGB = 23, 6, NT * IH, 3 * KD
    CAP = 64
    NP = E // 2

    with ExitStack() as ctx:
        def sb(name, shape, dt=F32):
            return ctx.enter_context(nc.sbuf_tensor(name, shape, dt))

        def sem(name):
            return ctx.enter_context(nc.semaphore(name))

        pb = ctx.enter_context(nc.psum_tensor("pb", [P, 8, 512], F32))

        ring = sb("ring", [P, RING, KD * SC])
        experts = sb("experts", [P, 2, 2, 3, KD * F])
        xs = sb("xs", [P, NT, D])
        uT = sb("uT", [P, KD, S])
        yacc = sb("yacc", [P, NT, D])
        ident = sb("ident", [P, P])
        perm = sb("perm", [P, 2, P])
        rope = sb("rope", [P, 4, S])
        ropei_tok = sb("ropei_tok", [P, 2, NT, ID // 2])
        masks = sb("masks", [P, 3, KALL])
        CAUSAL, DILATED, INDEXED = 0, 1, 2
        ones = sb("ones", [P, P])
        g_bc = sb("g_bc", [P, 2, D])
        modT = sb("modT", [P, 4, KD])
        adaT_bias = sb("adaT_bias", [P, L, 4, KD])
        ikgb = sb("ikgb", [P, L, 2, ID])
        rbias = sb("rbias", [P, L, E])
        silu_c = sb("silu_c", [P, 3, KD])
        acc = sb("acc", [P, 2, SC])
        sg = sb("sg", [P, 2, S])
        small = sb("small", [P, 64])
        stats = sb("stats", [P, 4, 6])
        negmax = sb("negmax", [P, 4, NT])
        esum = sb("esum", [P, 4, NT])
        rden = sb("rden", [P, 4, NT])
        gates = sb("gates", [P, NT, E])
        rt = sb("rt", [P, 5, NT, E])
        top8 = sb("top8", [P, NT, 8, 8])
        hbuf = sb("hbuf", [P, 4 * S])
        before = sb("before", [P, P])
        slots = sb("slots", [P, CAP])
        place = sb("place", [P, NT, E])
        flag = sb("flag", [P, 1], mybir.dt.int32)
        eh = sb("eh", [P, KF * S])
        powc = sb("powc", [P, 2])

        lend = experts[:, 1].rearrange("p e m n -> p (e m n)")
        at = [0]

        def part(*shape):
            n = 1
            for s in shape:
                n *= s
            a = lend[:, at[0]:at[0] + n]
            at[0] += n
            assert at[0] <= 2 * 3 * KD * F
            names = "abc"[:len(shape)]
            if len(shape) == 1:
                return a
            return a.rearrange(f"p ({' '.join(names)}) -> p {' '.join(names)}",
                               **{c: s for c, s in zip(names, shape)})

        qT = [part(4, S) for _ in range(3)]
        kT = [part(1, S), part(4, S), part(4, S)]
        v_a = part(NT, DH)
        v_b = part(NT, 512)
        v_c = part(NT, 512)
        oT = [part(4, S) for _ in range(3)]
        qiT = part(2, S)
        kiT = part(S)
        mergedT = lend[:, 0:KD * S].rearrange("p (k n) -> p k n", k=KD)
        score = hbuf[:, 0:KALL]
        relu = sg
        ki_tok = rt[:].rearrange("p a t e -> p (a t e)")
        lg = yacc[:].rearrange("p t d -> p (t d)")[:, 0:4 * KALL].rearrange("p (a n) -> p a n", a=4)
        pT = part(2, KALL)
        raw = eh[:].rearrange("p (a n) -> p a n", a=2)
        ropetmp = hbuf[:, 512:1024].rearrange("p (a n) -> p a n", a=2)
        hT = hbuf[:, 0:KF * S].rearrange("p (k n) -> p k n", k=KF)
        u_tok = uT[:].rearrange("p k n -> p (k n)").rearrange("p (t k c) -> p t k c", t=NT, k=KD)
        yflat = yacc[:].rearrange("p t d -> p (t d)")
        xg = yflat[:, 0:D].rearrange("p (k s) -> p k s", k=KD)
        ysb = yflat[:, D:2 * D]
        h_tok = hbuf[:, 0:F]
        hgT = hbuf[:, F:2 * F].rearrange("p (k s) -> p k s", k=KF)
        choose = hbuf[:, 2 * F:3 * F].rearrange("p (t s) -> p t s", t=NT)
        weigh = hbuf[:, 3 * F:4 * F].rearrange("p (t s) -> p t s", t=NT)
        weighT = eh[:].rearrange("p (a n) -> p a n", a=2)
        sig = sg[:, 0, :]

        ki_rows = sb("ki_rows", [P, NT, ID + IH])
        ki_tmp = sb("ki_tmp", [P, NT, ID])
        ki_prod = sb("ki_prod", [P, 4, NT, ID // 2])
        ki_done = sb("ki_done", [P, 1])
        wi = sb("wi", [P, NT, IH])
        mv = sb("mv", [P, NT, 2])
        gscore = sb("gscore", [P, 3, NT, 8])
        gsum = sb("gsum", [P, 2, NT])
        tmp_y = acc

        CONST_LOADS = [
            (xs[:], x.rearrange("(t p) d -> p t d", p=P)), (silu_c[:, 0, :], cT), (ident[:], ident_c), (perm[:], perm_c),
            (rope[:], rope_c), (ropei_tok[:], ropei_tok_c), (masks[:, 0:2, :], mask_c), (adaT_bias[:], adaT_b),
            (before[:], before_c), (slots[:], slot_c),
            (ikgb[:].rearrange("p l a i -> p (l a i)"), ik_gb.rearrange("l a i -> (l a i)").partition_broadcast(P)),
            (rbias[:].rearrange("p l e -> p (l e)"), router_bias.rearrange("l e -> (l e)").partition_broadcast(P)),
        ]
        N_CONSTS = len(CONST_LOADS)

        consts_landed = sem("consts_landed")
        ring_landed = [sem(f"ring_landed{i}") for i in range(RING)]
        gu_landed = [sem(f"gu_landed{i}") for i in range(2)]
        wd_landed = [sem(f"wd_landed{i}") for i in range(2)]
        gu_free = sem("gu_free")
        wd_free = sem("wd_free")
        gbias_landed = sem("gbias_landed")
        silu_exp = sem("silu_exp")
        silu_den = sem("silu_den")
        ones_ready = sem("ones_ready")
        acc_ready = sem("acc_ready")
        mod_done = sem("mod_done")
        mod_read = sem("mod_read")
        xT_done = sem("xT_done")
        uT_ready = sem("uT_ready")
        proj_done = sem("proj_done")
        raw_ready = sem("raw_ready")
        perm_done = sem("perm_done")
        rope_done = sem("rope_done")
        tok_done = sem("tok_done")
        tok_read = sem("tok_read")
        ki_ready = sem("ki_ready")
        kiT_done = sem("kiT_done")
        kiT_ready = sem("kiT_ready")
        idx_done = sem("idx_done")
        relu_ready = sem("relu_ready")
        score_used = sem("score_used")
        s_done = sem("s_done")
        max_ready = sem("max_ready")
        exp_done = sem("exp_done")
        p_ready = sem("p_ready")
        pt_done = sem("pt_done")
        pt_ready = sem("pt_ready")
        pv_done = sem("pv_done")
        o_read = sem("o_read")
        gb_done = sem("gb_done")
        eg_ready = sem("eg_ready")
        merged_done = sem("merged_done")
        y_done = sem("y_done")
        var_ready = sem("var_ready")
        rstd_ready = sem("rstd_ready")
        norm_done = sem("norm_done")
        router_done = sem("router_done")
        er_ready = sem("er_ready")
        sh_gu_done = sem("sh_gu_done")
        sh_exp = sem("sh_exp")
        sh_h = sem("sh_h")
        sh_down = sem("sh_down")
        chosen = sem("chosen")
        placed = sem("placed")
        flag_ready = sem("flag_ready")

        def per_layer(name):
            return [sem(f"{name}{l}") for l in range(L)]

        a_gu, a_exp, a_h, a_down, a_yacc, a_chain = (per_layer(n) for n in (
            "all_gu", "all_exp", "all_h", "all_down", "all_yacc", "all_chain"))
        utok_done, utok_ready = per_layer("utok_done"), per_layer("utok_ready")
        choose_ready, weigh_ready = per_layer("choose_ready"), per_layer("weigh_ready")
        xg_done, xg0_ready, xg1_ready = per_layer("xg_done"), per_layer("xg0_ready"), per_layer("xg1_ready")
        sig_ready, h_tok_ready = per_layer("sig_ready"), per_layer("h_tok_ready")
        turned, hgT_ready, weighT_ready = per_layer("turned"), per_layer("hgT_ready"), per_layer("weighT_ready")
        y0_done, y0_read, y1_read = per_layer("y0_done"), per_layer("y0_read"), per_layer("y1_read")
        scattered, c_chain = per_layer("scattered"), per_layer("compact_chain")
        yg_ready = sem("yg_ready")
        dve_chain = sem("dve_chain")
        pool_chain = sem("pool_chain")
        out_stored = sem("out_stored")

        class Chain:

            def __init__(self, eng, s):
                self.eng, self.s, self.n, self.turn = eng, s, 0, 0

            def __call__(self, ins):
                ins.then_inc(self.s, 1)
                self.n += 1
                self.eng.wait_ge(self.s, self.turn + self.n)

        def ring_slot(l, item):
            return (l * NI + WAVES[item]) % RING

        def ring_ap(l, item):
            return ring[:, ring_slot(l, item)]

        def dmas_upto(n_global):
            return sum(DMAS_OF.get(items[n % NI][0], 1) for n in range(n_global % RING, n_global + 1, RING))

        def wait_item(eng, l, item):
            n = l * NI + WAVES[item]
            eng.wait_ge(ring_landed[n % RING], 16 * dmas_upto(n))

        block = ctx.enter_context(nc.Block())

        @block.sync
        def _(sp):
            def used(n):
                l, (kind, j) = n // NI, items[n % NI]
                rope_at = {"qa": 4, "qb": 11, "kb": 15, "qc": 19, "kc": 23}
                tok_at = {"small": 2, "vb": 4, "vc": 6}
                if kind == "ada":
                    sp.wait_ge(acc_ready, N_ADA * l + j + 1)
                elif kind in rope_at:
                    sp.wait_ge(proj_done, NROPE * l + rope_at[kind])
                elif kind in tok_at:
                    sp.wait_ge(tok_done, NTOK * l + tok_at[kind])
                elif kind == "gate":
                    sp.wait_ge(gb_done, NGB * l + 4 * (j + 1))
                elif kind == "br":
                    sp.wait_ge(gb_done, NGB * l + KD * (j + 1))
                elif kind == "wout":
                    sp.wait_ge(y_done, 4 * l + 2 * (j + 1))
                elif kind == "ln":
                    sp.wait_ge(norm_done, 2 * l + j + 1)
                elif kind == "sh_gu":
                    sp.wait_ge(sh_gu_done, l + 1)
                else:
                    sp.wait_ge(sh_down, l + 1)

            def load_item(l, m):
                n = l * NI + m
                kind, j = items[m]
                if n >= RING:
                    used(n - RING)
                dst, s = ring[:, n % RING], ring_landed[n % RING]
                if kind == "ada":
                    sp.dma_start(dst.rearrange("p (k c) -> p k c", k=KD),
                                 ada_w[l, :, j * SC:(j + 1) * SC].rearrange("(p k) c -> p k c", k=KD)).then_inc(s, 16)
                elif kind in WIN_AT or kind == "gate":
                    c0 = WIN_AT[kind] if kind in WIN_AT else G_A + j * SC
                    w = SMALL if kind == "small" else SC
                    sp.dma_start(dst.rearrange("p (k c) -> p k c", k=KD)[:, :, 0:w],
                                 w_in[l, :, c0:c0 + w].rearrange("(p k) c -> p k c", k=KD)).then_inc(s, 16)
                elif kind == "br":
                    w = (w_br_a, w_br_b, w_br_c)[j]
                    sp.dma_start(dst.rearrange("p (b c) -> p b c", b=4),
                                 w[l].rearrange("(b p) c -> p b c", p=P)).then_inc(s, 16)
                elif kind == "wout":
                    sp.dma_start(dst.rearrange("p (k c) -> p k c", k=KD),
                                 w_out[l, :, j * SC:(j + 1) * SC].rearrange("(k p) c -> p k c", p=P)).then_inc(s, 16)
                elif kind == "ln":
                    for m in range(2):
                        sp.dma_start(dst[:, m * D:(m + 1) * D], ln_gb[l, j, m].partition_broadcast(P)).then_inc(s, 16)
                elif kind == "sh_gu":
                    sp.dma_start(dst[:, 0:KD * F], ws_gate[l].rearrange("(p k) c -> p (k c)", k=KD)).then_inc(s, 16)
                    sp.dma_start(dst[:, KD * F:2 * KD * F], ws_up[l].rearrange("(p k) c -> p (k c)", k=KD)).then_inc(s, 16)
                else:
                    sp.dma_start(dst[:, 0:KF * D], ws_down[l].rearrange("(p k) c -> p (k c)", k=KF)).then_inc(s, 16)
                    sp.dma_start(dst[:, KF * D:KF * D + KD * E],
                                 w_router[l].rearrange("(p k) c -> p (k c)", k=KD)).then_inc(s, 16)

            def load_pair(l, slot, e0, used=None):
                if used is not None:
                    sp.wait_ge(gu_free, used)
                for m, w in enumerate((w_gate, w_up)):
                    sp.dma_start(experts[:, slot, :, m, :],
                                 w[l, bass.ds(e0, 2)].rearrange("e (p k) c -> p e (k c)", k=KD)).then_inc(gu_landed[slot], 16)
                if used is not None:
                    sp.wait_ge(wd_free, used)
                sp.dma_start(experts[:, slot, :, 2, :],
                             w_down[l, bass.ds(e0, 2)].rearrange("e (p k) c -> p e (k c)", k=KF)).then_inc(wd_landed[slot], 16)

            EARLY = 2
            for l in range(L):
                for m in range(EARLY if l else 0, NI):
                    load_item(l, m)
                    if items[m] == ("vc", 0):
                        load_pair(l, 0, 0, NP * l if l else None)
                sp.wait_ge(y_done, 4 * (l + 1))
                load_pair(l, 1, 2)
                if l < L - 1:
                    for m in range(EARLY):
                        load_item(l + 1, m)
                with sp.Fori(1, NP // 2) as i:
                    for slot in range(2):
                        load_pair(l, slot, i * 4 + 2 * slot, i * 2 + (NP * l + slot - 1))
            sp.wait_ge(norm_done, 2 * L)
            sp.dma_start(out.rearrange("(t p) d -> p t d", p=P), xs[:]).then_inc(out_stored, 16)
            sp.wait_ge(out_stored, 16)

        @block.gpsimd
        def _(pool):
            nc.gpsimd.memset(powc[:], -0.5).then_inc(pool_chain, 1)
            pool.wait_ge(pool_chain, 1)

            def rstd(n):
                pool.wait_ge(var_ready, n)
                nc.gpsimd.tensor_tensor(small[:, 4:6], small[:, 2:4], powc[:], ALU.pow).then_inc(rstd_ready, 1)

            for l in range(L):
                if l:
                    pool.wait_ge(norm_done, 2 * l)
                for m, piece in enumerate((2, 5)):
                    pool.dma_start(g_bc[:, m, :], ada_b[l, piece * D:(piece + 1) * D].partition_broadcast(P))\
                        .then_inc(gbias_landed, 16)
                for n in range(3):
                    rstd(3 * l + n + 1)

        @block.tensor
        def _(pe):
            mm = nc.tensor.matmul

            def transpose_x(n):
                for k in range(KD):
                    for t in range(NT):
                        o = (k % 2) * S + t * P
                        ins = nc.tensor.transpose(pb[:, k // 2, o:o + P], xs[:, t, k::KD], ident[:])
                    if k % 2:
                        ins.then_inc(xT_done, 1)

            def contract(dst, lhs, rhs, n):
                for k in range(n):
                    ins = mm(dst, lhs(k), rhs(k), start=(k == 0), stop=(k == n - 1))
                return ins

            def modulation(l):
                for j in range(N_ADA):
                    pe.wait_ge(acc_ready, N_ADA * l + j + 1)
                    if j >= 2:
                        pe.wait_ge(mod_read, N_ADA * l + j - 1)
                    if j // 2 in (2, 5):
                        ins = mm(pb[:, 5 + j % 2, :], ones[:], acc[:, j % 2, :], start=True, stop=True)
                    else:
                        q = (0, 1, None, 2, 3)[j // 2]
                        h = 64 * (j % 2)
                        for k in range(KD):
                            ins = mm(pb[h:h + 64, 7, q * KD + k:q * KD + k + 1], acc[:, j % 2, k::KD], ones[:, 0:1],
                                     start=True, stop=True)
                    ins.then_inc(mod_done, 1)

            def rotate_half(r, l):
                pe.wait_ge(raw_ready, NROPE * l + r + 1)
                if r >= 2:
                    pe.wait_ge(rope_done, NROPE * l + r - 1)
                mm(pb[:, 2 + r % 2, 0:S], perm[:, 1 if r in (5, 6) else 0, :], raw[:, r % 2, :], start=True, stop=True)\
                    .then_inc(perm_done, 1)

            def projections(l):
                r = 0
                for name, blocks in (("qa", 4), ("small", 3), ("qb", 4), ("kb", 4), ("vb", 0), ("qc", 4), ("kc", 4), ("vc", 0)):
                    wait_item(pe, l, (name, 0))
                    w = ring_ap(l, (name, 0)).rearrange("p (k c) -> p k c", k=KD)
                    for b in range(blocks):
                        if r >= 2:
                            pe.wait_ge(raw_ready, NROPE * l + r - 1)
                        if name == "small" and b == 0:
                            for h in range(2):
                                ins = contract(pb[64 * h:64 * h + 64, r % 2, 0:S], lambda k: w[:, k, 0:DH],
                                               lambda k: uT[:, k, :], KD)
                        else:
                            c0 = b * P if name != "small" else 2 * DH + (b - 1) * P
                            ins = contract(pb[:, r % 2, 0:S], lambda k: w[:, k, c0:c0 + P], lambda k: uT[:, k, :], KD)
                        ins.then_inc(proj_done, 1)
                        if r:
                            rotate_half(r - 1, l)
                        r += 1
                    if name in ("small", "vb", "vc"):
                        g = ("small", "vb", "vc").index(name)
                        for t in range(NT):
                            if g:
                                pe.wait_ge(tok_read, NTOK * l + 2 * (g - 1) + t + 1)
                            lhs = lambda k: uT[:, k, t * P:(t + 1) * P]
                            if g == 0:
                                contract(pb[:, 4 + t, 0:DH], lhs, lambda k: w[:, k, DH:2 * DH], KD)
                                ins = contract(pb[:, 4 + t, DH:DH + ID + IH], lhs, lambda k: w[:, k, 384:384 + ID + IH], KD)
                            else:
                                ins = contract(pb[:, 4 + t, :], lhs, lambda k: w[:, k, :], KD)
                            ins.then_inc(tok_done, 1)
                rotate_half(r - 1, l)

            def indexer(l):
                pe.wait_ge(ki_ready, l + 1)
                for t in range(NT):
                    ins = nc.tensor.transpose(pb[:, 6, t * P:(t + 1) * P], ki_tok[:, t * P:(t + 1) * P], ident[:])
                ins.then_inc(kiT_done, 1)
                pe.wait_ge(kiT_ready, l + 1)
                pe.wait_ge(rope_done, NROPE * (l + 1))
                pe.wait_ge(tok_read, NTOK * (l + 1))
                i = 0
                for t in range(NT):
                    for h in range(IH):
                        if i >= 2:
                            pe.wait_ge(relu_ready, NIDX * l + i - 1)
                        r = ID * (h % 4)
                        mm(pb[:, 4 + i % 2, 0:KEYS[t]], qiT[r:r + ID, h // 4, t * P:(t + 1) * P], kiT[r:r + ID, 0:KEYS[t]],
                           start=True, stop=True, tile_position=(r, 0)).then_inc(idx_done, 1)
                        i += 1

            ORDER = [(br, h) for br in (1, 2, 0) for h in range(8)]

            def scores(l, i):
                br, h = ORDER[i]
                r = DH * (h % 2)
                if i >= 2:
                    pe.wait_ge(max_ready, HC * l + i - 1)
                for t in range(NT):
                    ins = mm(pb[:, i % 2, KOFF[t]:KOFF[t] + KEYS[t]], qT[br][r:r + DH, h // 2, t * P:(t + 1) * P],
                             kT[br][r:r + DH, (h // 2 if br else 0), 0:KEYS[t]], start=True, stop=True)
                ins.then_inc(s_done, 1)

            def turn_probs(l, i):
                pe.wait_ge(p_ready, HC * l + i + 1)
                if i >= 2:
                    pe.wait_ge(pt_ready, HC * l + i - 1)
                for m in range(3):
                    ins = nc.tensor.transpose(pb[:, 2 + i % 2, m * P:(m + 1) * P], lg[:, i % 4, m * P:(m + 1) * P], ident[:])
                ins.then_inc(pt_done, 1)

            def values(l, i):
                br, h = ORDER[i]
                hp = i // 2
                pe.wait_ge(pt_ready, HC * l + i + 1)
                if i % 2 == 0 and hp >= 2:
                    pe.wait_ge(o_read, HC // 2 * l + hp - 1)
                v = (v_a, v_b, v_c)[br]
                c = 0 if br == 0 else h * DH
                o = pb[DH * (h % 2):DH * (h % 2) + DH, 4 + hp % 2, 0:S]
                mm(o, v[:, 0, c:c + DH], pT[:, i % 2, 0:S], start=True, stop=False)
                mm(o[:, P:S], v[:, 1, c:c + DH], pT[:, i % 2, S:S + P], start=False, stop=True).then_inc(pv_done, 1)

            def attention(l):
                for i in range(HC + 3):
                    if i < HC:
                        scores(l, i)
                    if 2 <= i < HC + 2:
                        turn_probs(l, i - 2)
                    if 3 <= i:
                        values(l, i - 3)

            def branches(l):
                pe.wait_ge(o_read, HC // 2 * (l + 1))
                for br in range(3):
                    wait_item(pe, l, ("br", br))
                    wb = ring_ap(l, ("br", br)).rearrange("p (b c) -> p b c", b=4)
                    for k in range(KD):
                        j = br * KD + k
                        if k % 4 == 0:
                            wait_item(pe, l, ("gate", 2 * br + k // 4))
                        wg = ring_ap(l, ("gate", 2 * br + k // 4)).rearrange("p (k c) -> p k c", k=KD)
                        if j >= 2:
                            pe.wait_ge(merged_done, NGB * l + j - 1)
                        contract(pb[:, 2 + j % 2, 0:S], lambda b: wb[:, b, k * P:(k + 1) * P], lambda b: oT[br][:, b, :], 4)
                        contract(pb[:, j % 2, 0:S], lambda q: wg[:, q, (k % 4) * P:(k % 4 + 1) * P],
                                 lambda q: uT[:, q, :], KD).then_inc(gb_done, 1)

            def mix_out(l):
                pe.wait_ge(merged_done, NGB * (l + 1))
                for half in range(2):
                    wait_item(pe, l, ("wout", half))
                    w = ring_ap(l, ("wout", half)).rearrange("p (k c) -> p k c", k=KD)
                    for t in range(NT):
                        contract(pb[:, 4 + 2 * half + t, :], lambda k: mergedT[:, k, t * P:(t + 1) * P],
                                 lambda k: w[:, k, :], KD).then_inc(y_done, 1)

            def router(l):
                wait_item(pe, l, ("sh_d", 0))
                w = ring_ap(l, ("sh_d", 0))[:, KF * D:KF * D + KD * E].rearrange("p (k c) -> p k c", k=KD)
                pe.wait_ge(uT_ready, 2 * KD * (l + 1))
                for t in range(NT):
                    ins = contract(pb[:, 2, t * E:(t + 1) * E], lambda k: uT[:, k, t * P:(t + 1) * P], lambda k: w[:, k, :], KD)
                ins.then_inc(router_done, 1)
                pe.wait_ge(er_ready, l + 1)

            def gate_up(wg, wu, done):
                for q, w in enumerate((wg, wu)):
                    for m in range(KF):
                        ins = contract(pb[:, q, m * S:(m + 1) * S], lambda k: w[:, k, m::KF], lambda k: uT[:, k, :], KD)
                ins.then_inc(done, 1)

            def down(wd, done):
                for t in range(NT):
                    for half in range(2):
                        ins = contract(pb[:, 4 + 2 * half + t, :], lambda k: hT[:, k, t * P:(t + 1) * P],
                                       lambda k: wd[:, k, half * 512:(half + 1) * 512], KF)
                ins.then_inc(done, 1)

            def places(l):
                sel = rt[:, 4]
                pe.wait_ge(chosen, l + 1)
                mm(pb[:, 3, 0:E], before[:], sel[:, 0, :], start=True, stop=True)
                mm(pb[:, 3, E:2 * E], before[:], sel[:, 1, :], start=True, stop=False)
                mm(pb[:, 3, E:2 * E], ones[:], sel[:, 0, :], start=False, stop=True)
                mm(pb[:, 3, 2 * E:3 * E], ones[:], sel[:, 0, :], start=True, stop=False)
                mm(pb[:, 3, 2 * E:3 * E], ones[:], sel[:, 1, :], start=False, stop=True).then_inc(placed, 1)

            def all_tokens(l):
                with pe.Fori(0, E // 4) as i:
                    for e in range(4):
                        slot = e // 2
                        w = experts[:, slot, e % 2]
                        if e % 2 == 0:
                            pe.wait_ge(gu_landed[slot], i * 32 + (32 * (E // 4) * l + 32))
                            pe.wait_ge(wd_landed[slot], i * 16 + (16 * (E // 4) * l + 16))
                        gate_up(w[:, 0, :].rearrange("p (k c) -> p k c", k=KD), w[:, 1, :].rearrange("p (k c) -> p k c", k=KD),
                                a_gu[l])
                        pe.wait_ge(a_h[l], i * 4 + (e + 1))
                        pe.wait_ge(a_yacc[l], i * 4 + (e + 1))
                        down(w[:, 2, :].rearrange("p (k c) -> p k c", k=KF), a_down[l])

            def compact(l):
                for k in range(KD):
                    for t in range(NT):
                        o = (k % 4) * P
                        ins = nc.tensor.transpose(pb[:, 2 * t + k // 4, o:o + P], uT[:, k, t * P:(t + 1) * P], ident[:])
                ins.then_inc(utok_done[l], 1)
                pe.wait_ge(utok_ready[l], 2)

                def gather(n, read):
                    pe.wait_ge(choose_ready[l], n)
                    for k in range(KD):
                        if read is not None and k % 4 == 0:
                            pe.wait_ge((y0_read, y1_read)[k // 4][l], read)
                        ins = contract(pb[:, k // 4, (k % 4) * P:(k % 4 + 1) * P], lambda t: u_tok[:, t, k, :],
                                       lambda t: choose[:, t, :], NT)
                        if k % 4 == 3:
                            ins.then_inc(xg_done[l], 1)

                def up(n, slot, landed):
                    pe.wait_ge(xg0_ready[l], n)
                    pe.wait_ge(gu_landed[slot], landed)
                    for k in range(KD):
                        if k == 4:
                            pe.wait_ge(xg1_ready[l], n)
                        for e in range(2):
                            ins = mm(pb[64 * e:64 * e + 64, 2, :], xg[:, k, CAP * e:CAP * (e + 1)],
                                     experts[:, slot, e, 0:2, k * F:(k + 1) * F], start=(k == 0), stop=(k == KD - 1))
                    ins.then_inc(gu_free, 1)

                def turn(n, read):
                    pe.wait_ge(h_tok_ready[l], n)
                    pe.wait_ge(weigh_ready[l], n)
                    if read is not None:
                        pe.wait_ge(weighT_ready[l], read)
                    for k in range(KF):
                        nc.tensor.transpose(pb[:, 3, k * P:(k + 1) * P], h_tok[:, k::KF], ident[:])
                    for t in range(NT):
                        ins = nc.tensor.transpose(pb[:, 3, S + t * P:S + (t + 1) * P], weigh[:, t, :], ident[:])
                    ins.then_inc(turned[l], 1)

                def scatter(n, parity, last=False):
                    pe.wait_ge(weighT_ready[l], n)
                    for half in range(2):
                        pe.wait_ge((y0_read, y1_read)[half][l], n)
                        for t in range(NT):
                            ins = mm(pb[:, 4 + 2 * half + t, :], weighT[:, parity, t * P:(t + 1) * P],
                                     ysb[:, half * 512:(half + 1) * 512], start=False, stop=True, skip_group_check=True)
                    if last:
                        ins.then_inc(scattered[l], 1)

                def down_pair(n, slot, landed, bank_read):
                    pe.wait_ge(hgT_ready[l], n)
                    pe.wait_ge(wd_landed[slot], landed)
                    for half in range(2):
                        pe.wait_ge((xg0_ready, xg1_ready)[half][l], bank_read)
                        for k in range(KF):
                            for e in range(2):
                                ins = mm(pb[64 * e:64 * e + 64, half, :], hgT[:, k, CAP * e:CAP * (e + 1)],
                                         experts[:, slot, e, 2, k * D + half * 512:k * D + (half + 1) * 512],
                                         start=(k == 0), stop=(k == KF - 1))
                        ins.then_inc(wd_free if half else y0_done[l], 1)

                GU0, WD0 = 32 * (NP // 2) * l, 16 * (NP // 2) * l

                def step(i, q, first=False, last=False):
                    n = i * 2 + (q + 1)
                    if not last:
                        gather(n + 1, None if first else n - 1)
                    turn(n, None if first else n - 1)
                    if not first:
                        scatter(n - 1, (q + 1) % 2)
                    down_pair(n, q % 2, i * 16 + (WD0 + 16 * (q // 2 + 1)), n if last else n + 1)
                    if not last:
                        up(n + 1, (q + 1) % 2, i * 32 + (GU0 + 32 * ((q + 1) // 2 + 1)))

                gather(1, None)
                up(1, 0, GU0 + 32)
                step(0, 0, first=True)
                with pe.Fori(0, (NP - 4) // 2) as i:
                    step(i, 1)
                    step(i, 2)
                for p in range(NP - 3, NP):
                    step(p // 2, p % 2, last=(p == NP - 1))
                scatter(NP, (NP - 1) % 2, last=True)

            for l in range(L):
                pe.wait_ge(consts_landed, 16 * N_CONSTS)
                pe.wait_ge(ones_ready, 1)
                if l:
                    pe.wait_ge(norm_done, 2 * l)
                modulation(l)
                transpose_x(2 * l)
                pe.wait_ge(uT_ready, KD * (2 * l + 1))
                pe.wait_ge(mod_read, N_ADA * (l + 1))
                projections(l)
                indexer(l)
                attention(l)
                branches(l)
                mix_out(l)
                pe.wait_ge(norm_done, 2 * l + 1)
                transpose_x(2 * l + 1)
                router(l)
                wait_item(pe, l, ("sh_gu", 0))
                w = ring_ap(l, ("sh_gu", 0))
                gate_up(w[:, 0:KD * F].rearrange("p (k c) -> p k c", k=KD),
                        w[:, KD * F:2 * KD * F].rearrange("p (k c) -> p k c", k=KD), sh_gu_done)
                pe.wait_ge(sh_h, l + 1)
                down(ring_ap(l, ("sh_d", 0))[:, 0:KF * D].rearrange("p (k c) -> p k c", k=KF), sh_down)
                places(l)
                pe.wait_ge(flag_ready, l + 1)
                crowded = pe.value_load(flag[0:1, 0:1], min_val=0, max_val=1)
                with pe.If(crowded > 0):
                    all_tokens(l)
                with pe.Else():
                    compact(l)

        @block.scalar
        def _(act):
            def cp(dst, src):
                return nc.scalar.copy(dst, src)

            for dst, src in CONST_LOADS:
                act.dma_start(dst, src).then_inc(consts_landed, 16)
            act.wait_ge(consts_landed, 16 * N_CONSTS)
            nc.scalar.activation(silu_c[:, 1, :], silu_c[:, 0, :], ACT.Exp, scale=-1.0).then_inc(silu_exp, 1)

            def rotary(l, r):
                act.wait_ge(proj_done, NROPE * l + r + 1)
                if r >= 2:
                    act.wait_ge(rope_done, NROPE * l + r - 1)
                cp(raw[:, r % 2, :], pb[:, r % 2, 0:S]).then_inc(raw_ready, 1)

            def token_rows(l, g):
                for t in range(NT):
                    act.wait_ge(tok_done, NTOK * l + 2 * g + t + 1)
                    if g == 0:
                        cp(v_a[:, t, :], pb[:, 4 + t, 0:DH])
                        cp(ki_rows[:, t, :], pb[:, 4 + t, DH:DH + ID + IH]).then_inc(tok_read, 1)
                    else:
                        cp((v_b, v_c)[g - 1][:, t, :], pb[:, 4 + t, :]).then_inc(tok_read, 1)

            def soft(l, i):
                act.wait_ge(max_ready, HC * l + i + 1)
                for t in range(NT):
                    a = lg[:, i % 4, KOFF[t]:KOFF[t] + KEYS[t]]
                    ins = nc.scalar.activation(a, a, ACT.Exp, bias=negmax[:, i % 4, t:t + 1],
                                               accum_out=esum[:, i % 4, t:t + 1])
                ins.then_inc(exp_done, 1)

            def probs_out(l, i):
                act.wait_ge(pt_done, HC * l + i + 1)
                if i >= 2:
                    act.wait_ge(pv_done, HC * l + i - 1)
                cp(pT[:, i % 2, :], pb[:, 2 + i % 2, 0:KALL]).then_inc(pt_ready, 1)

            def heads_out(l, hp):
                act.wait_ge(pv_done, HC * l + 2 * hp + 2)
                br = (1, 2, 0)[hp // 4]
                cp(oT[br][:, hp % 4, :], pb[:, 4 + hp % 2, 0:S]).then_inc(o_read, 1)

            def all_tokens(l):
                with act.Fori(0, E // 4) as i:
                    for e in range(4):
                        act.wait_ge(a_gu[l], i * 4 + (e + 1))
                        if e % 2:
                            act.sem_inc(gu_free, 1)
                        nc.scalar.activation(eh[:], pb[:, 0, :], ACT.Exp, scale=-1.0).then_inc(a_exp[l], 1)
                        if e % 2:
                            act.wait_ge(a_down[l], i * 4 + (e + 1))
                            act.sem_inc(wd_free, 1)

            def compact(l):
                act.wait_ge(utok_done[l], 1)
                cp(u_tok[:, 0].rearrange("p k c -> p (k c)"), pb[:, 0:2, :].rearrange("p b n -> p (b n)")).then_inc(utok_ready[l], 1)

                def gathered(n):
                    act.wait_ge(xg_done[l], n * 2 - 1)
                    cp(xg[:, 0:4, :].rearrange("p k s -> p (k s)"), pb[:, 0, :]).then_inc(xg0_ready[l], 1)

                def step(i, q, last=False):
                    n = i * 2 + (q + 1)
                    act.wait_ge(gu_free, i * 2 + (NP * l + q + 1))
                    nc.scalar.activation(sig, pb[:, 2, 0:F], ACT.Exp, scale=-1.0).then_inc(sig_ready[l], 1)
                    if not last:
                        gathered(n + 1)
                    act.wait_ge(turned[l], n)
                    cp(hgT.rearrange("p k s -> p (k s)"), pb[:, 3, 0:F]).then_inc(hgT_ready[l], 1)
                    cp(weighT[:, q % 2, :], pb[:, 3, F:2 * F]).then_inc(weighT_ready[l], 1)
                    act.wait_ge(y0_done[l], n)
                    cp(ysb[:, 0:512], pb[:, 0, :]).then_inc(y0_read[l], 1)

                gathered(1)
                step(0, 0)
                with act.Fori(0, (NP - 4) // 2) as i:
                    step(i, 1)
                    step(i, 2)
                for p in range(NP - 3, NP):
                    step(p // 2, p % 2, last=(p == NP - 1))

            for l in range(L):
                r = 0
                for blocks, tok in ((7, 0), (8, 1), (8, 2)):
                    for _ in range(blocks):
                        rotary(l, r)
                        r += 1
                    token_rows(l, tok)
                act.wait_ge(kiT_done, l + 1)
                cp(kiT, pb[:, 6, 0:S]).then_inc(kiT_ready, 1)
                i = 0
                for t in range(NT):
                    for h in range(IH):
                        act.wait_ge(idx_done, NIDX * l + i + 1)
                        if i >= 2:
                            act.wait_ge(score_used, NIDX * l + i - 1)
                        nc.scalar.activation(relu[:, i % 2, 0:KEYS[t]], pb[:, 4 + i % 2, 0:KEYS[t]], ACT.Relu,
                                             scale=float(ID) ** -0.5).then_inc(relu_ready, 1)
                        i += 1
                for i in range(HC + 3):
                    if i < HC:
                        soft(l, i)
                    if 2 <= i < HC + 2:
                        probs_out(l, i - 2)
                    if i >= 4 and i % 2 == 0:
                        heads_out(l, (i - 4) // 2)
                for j in range(NGB):
                    act.wait_ge(gb_done, NGB * l + j + 1)
                    if j >= 2:
                        act.wait_ge(merged_done, NGB * l + j - 1)
                    nc.scalar.activation(sg[:, j % 2, :], pb[:, j % 2, 0:S], ACT.Exp, scale=-1.0).then_inc(eg_ready, 1)
                act.wait_ge(router_done, l + 1)
                nc.scalar.activation(rt[:, 0, :, :], pb[:, 2, 0:NT * E].rearrange("p (t e) -> p t e", t=NT), ACT.Exp,
                                     scale=-1.0).then_inc(er_ready, 1)
                act.wait_ge(sh_gu_done, l + 1)
                nc.scalar.activation(eh[:], pb[:, 0, :], ACT.Exp, scale=-1.0).then_inc(sh_exp, 1)
                act.wait_ge(flag_ready, l + 1)
                crowded = act.value_load(flag[0:1, 0:1], min_val=0, max_val=1)
                with act.If(crowded > 0):
                    all_tokens(l)
                with act.Else():
                    compact(l)

        @block.vector
        def _(dve):
            v = nc.vector
            link = Chain(dve, dve_chain)
            v.memset(ones[:], 1.0).then_inc(ones_ready, 1)
            dve.wait_ge(consts_landed, 16 * N_CONSTS)
            dve.wait_ge(silu_exp, 1)
            link(v.tensor_scalar(silu_c[:, 1, :], silu_c[:, 1, :], 1.0, None, ALU.add))
            link(v.reciprocal(silu_c[:, 2, :], silu_c[:, 1, :]))
            link(v.tensor_tensor(silu_c[:, 1, :], silu_c[:, 0, :], silu_c[:, 2, :], ALU.mult))

            def mod_evacuate(l, j):
                dve.wait_ge(mod_done, N_ADA * l + j + 1)
                piece, half = j // 2, j % 2
                if piece in (2, 5):
                    q = (piece - 2) // 3
                    if piece == 2 and half == 0:
                        dve.wait_ge(gbias_landed, 32 * (l + 1))
                    a = g_bc[:, q, half * SC:(half + 1) * SC]
                    v.scalar_tensor_tensor(a, pb[:, 5 + half, :], 1.0, a, ALU.add, ALU.add).then_inc(mod_read, 1)
                else:
                    q = (0, 1, None, 2, 3)[piece]
                    h = slice(64 * half, 64 * half + 64)
                    v.scalar_tensor_tensor(modT[h, q, :], pb[h, 7, q * KD:(q + 1) * KD], float(q % 2),
                                           adaT_bias[h, l, q, :], ALU.add, ALU.add).then_inc(mod_read, 1)

            def modulation(l):
                for j in range(N_ADA):
                    wait_item(dve, l, ("ada", j))
                    w = ring_ap(l, ("ada", j)).rearrange("p (k c) -> p k c", k=KD)
                    if j >= 2:
                        dve.wait_ge(mod_done, N_ADA * l + j - 1)
                    a = acc[:, j % 2, :]
                    link(v.tensor_scalar(a, w[:, 0, :], silu_c[:, 1, 0:1], None, ALU.mult))
                    for k in range(1, KD):
                        ins = v.scalar_tensor_tensor(a, w[:, k, :], silu_c[:, 1, k:k + 1], a, ALU.mult, ALU.add)
                        if k < KD - 1:
                            link(ins)
                    ins.then_inc(acc_ready, 1)
                    if j:
                        mod_evacuate(l, j - 1)
                mod_evacuate(l, N_ADA - 1)
                dve.wait_ge(mod_read, N_ADA * (l + 1))

            def modulate(n):
                for k in range(KD):
                    dve.wait_ge(xT_done, KD // 2 * n + k // 2 + 1)
                    q = 2 * (n % 2)
                    v.tensor_scalar(uT[:, k, :], pb[:, k // 2, (k % 2) * S:(k % 2 + 1) * S], modT[:, q + 1, k:k + 1],
                                    modT[:, q, k:k + 1], ALU.mult, ALU.add).then_inc(uT_ready, 1)

            ROPE_DST = [qT[0][:, b, :] for b in range(4)] + [kT[0][:, 0, :]] + [qiT[:, b, :] for b in range(2)]
            for br in (1, 2):
                ROPE_DST += [qT[br][:, b, :] for b in range(4)] + [kT[br][:, b, :] for b in range(4)]

            def rotary(l, r):
                q = 2 if r in (5, 6) else 0
                dve.wait_ge(raw_ready, NROPE * l + r + 1)
                if r:
                    dve.wait_ge(rope_done, NROPE * l + r)
                v.tensor_tensor(ropetmp[:, 0, :], raw[:, r % 2, :], rope[:, q, :], ALU.mult)
                dve.wait_ge(perm_done, NROPE * l + r + 1)
                link(v.tensor_tensor(ropetmp[:, 1, :], pb[:, 2 + r % 2, 0:S], rope[:, q + 1, :], ALU.mult))
                v.tensor_tensor(ROPE_DST[r], ropetmp[:, 0, :], ropetmp[:, 1, :], ALU.add).then_inc(rope_done, 1)

            def indexer_keys(l):
                dve.wait_ge(tok_read, NTOK * l + 2)
                for t in range(NT):
                    ins = v.bn_stats(stats[:, t, :], ki_rows[:, t, 0:ID])
                link(ins)
                for t in range(NT):
                    ins = v.bn_aggr(mv[:, t, :], stats[:, t, :])
                link(ins)
                v.tensor_scalar(small[:, 2:4], mv[:, :, 1], EPS, None, ALU.add).then_inc(var_ready, 1)
                dve.wait_ge(rstd_ready, 3 * l + 1)
                kn = ki_tmp
                for t in range(NT):
                    ins = v.tensor_scalar(kn[:, t, :], ki_rows[:, t, 0:ID], mv[:, t, 0:1], small[:, 4 + t:5 + t],
                                          ALU.subtract, ALU.mult)
                link(ins)
                for t in range(NT):
                    ins = v.tensor_tensor(kn[:, t, :], kn[:, t, :], ikgb[:, l, 0, :], ALU.mult)
                link(ins)
                for t in range(NT):
                    ins = v.tensor_tensor(kn[:, t, :], kn[:, t, :], ikgb[:, l, 1, :], ALU.add)
                link(ins)
                H = ID // 2
                x1, x2 = kn[:, :, 0:H], kn[:, :, H:ID]
                v.tensor_tensor(ki_prod[:, 0], x1, ropei_tok[:, 0], ALU.mult)
                v.tensor_tensor(ki_prod[:, 1], x2, ropei_tok[:, 1], ALU.mult)
                v.tensor_tensor(ki_prod[:, 2], x2, ropei_tok[:, 0], ALU.mult)
                link(v.tensor_tensor(ki_prod[:, 3], x1, ropei_tok[:, 1], ALU.mult))
                dst = ki_tok[:, 0:NT * P].rearrange("p (t c i) -> p t c i", t=NT, c=4)
                for c in range(4):
                    v.tensor_tensor(dst[:, :, c, 0:H], ki_prod[:, 0], ki_prod[:, 1], ALU.subtract)
                    ins = v.tensor_tensor(dst[:, :, c, H:ID], ki_prod[:, 2], ki_prod[:, 3], ALU.add)
                link(v.tensor_scalar(wi[:], ki_rows[:, :, ID:ID + IH], float(IH) ** -0.5, None, ALU.mult))
                ins = v.tensor_copy(ki_done[:], wi[:, 0, 0:1])
                ins.then_inc(ki_ready, 1)

            def indexer(l):
                i = 0
                for t in range(NT):
                    o = slice(KOFF[t], KOFF[t] + KEYS[t])
                    for h in range(IH):
                        dve.wait_ge(relu_ready, NIDX * l + i + 1)
                        other = masks[:, CAUSAL, o] if h == 0 else score[:, o]
                        v.scalar_tensor_tensor(score[:, o], relu[:, i % 2, 0:KEYS[t]], wi[:, t, h:h + 1], other,
                                               ALU.mult, ALU.add).then_inc(score_used, 1)
                        i += 1
                        dve.wait_ge(score_used, NIDX * l + i)
                for n in range(TOPK_ROUNDS):
                    for t in range(NT):
                        o = slice(KOFF[t], KOFF[t] + KEYS[t])
                        ins = v.max(top8[:, t, n, :], score[:, o])
                    link(ins)
                    for t in range(NT):
                        o = slice(KOFF[t], KOFF[t] + KEYS[t])
                        ins = v.match_replace(score[:, o], top8[:, t, n, :], score[:, o], NEG)
                    link(ins)
                link(v.tensor_scalar(masks[:, INDEXED, :], score, SELECTED, NEG, ALU.is_ge, ALU.mult))
                link(v.tensor_tensor(masks[:, INDEXED, :], masks[:, INDEXED, :], masks[:, CAUSAL, :], ALU.add))

            MASK_OF = (DILATED, CAUSAL, INDEXED)

            def logits(l, i):
                dve.wait_ge(s_done, HC * l + i + 1)
                if i >= 4:
                    dve.wait_ge(pt_done, HC * l + i - 3)
                link(v.scalar_tensor_tensor(lg[:, i % 4, :], pb[:, i % 2, 0:KALL], SCALE, masks[:, MASK_OF[i // 8], :],
                                            ALU.mult, ALU.add))
                for t in range(NT):
                    ins = v.tensor_reduce(negmax[:, i % 4, t:t + 1], lg[:, i % 4, KOFF[t]:KOFF[t] + KEYS[t]], AX.X, ALU.max,
                                          negate=True)
                ins.then_inc(max_ready, 1)

            def normalise(l, i):
                dve.wait_ge(exp_done, HC * l + i + 1)
                link(v.reciprocal(rden[:, i % 4, :], esum[:, i % 4, :]))
                for t in range(NT):
                    a = lg[:, i % 4, KOFF[t]:KOFF[t] + KEYS[t]]
                    ins = v.tensor_scalar(a, a, rden[:, i % 4, t:t + 1], None, ALU.mult)
                ins.then_inc(p_ready, 1)

            def sigmoid_den(a, link=link):
                link(v.tensor_scalar(a, a, 1.0, None, ALU.add))
                link(v.reciprocal(a, a))

            def merge(l):
                for j in range(NGB):
                    dve.wait_ge(eg_ready, NGB * l + j + 1)
                    a = sg[:, j % 2, :]
                    sigmoid_den(a)
                    m = mergedT[:, j % KD, :]
                    if j < KD:
                        v.tensor_tensor(m, a, pb[:, 2 + j % 2, 0:S], ALU.mult).then_inc(merged_done, 1)
                    else:
                        link(v.tensor_tensor(a, a, pb[:, 2 + j % 2, 0:S], ALU.mult))
                        v.tensor_tensor(m, m, a, ALU.add).then_inc(merged_done, 1)
                dve.wait_ge(merged_done, NGB * (l + 1))

            PARTS = [(t, half) for half in range(2) for t in range(NT)]

            def norm(n, weighted=False):
                for t, half in PARTS:
                    o = slice(half * 512, half * 512 + 512)
                    if weighted:
                        gy = yacc[:, t, o]
                    else:
                        gy = tmp_y[:, (2 * half + t) % 2, :]
                        link(v.tensor_tensor(gy, pb[:, 4 + 2 * half + t, :], g_bc[:, n % 2, o], ALU.mult))
                    link(v.scalar_tensor_tensor(xs[:, t, o], xs[:, t, o], ALPHA, gy, ALU.mult, ALU.add))
                    link(v.bn_stats(stats[:, 2 * t + half, :], xs[:, t, o]))
                for t in range(NT):
                    ins = v.bn_aggr(mv[:, t, :], stats[:, 2 * t:2 * t + 2, :])
                link(ins)
                v.tensor_scalar(small[:, 2:4], mv[:, :, 1], EPS, None, ALU.add).then_inc(var_ready, 1)
                dve.wait_ge(rstd_ready, 3 * (n // 2) + 2 + n % 2)
                wait_item(dve, n // 2, ("ln", n % 2))
                ln_bc = ring_ap(n // 2, ("ln", n % 2))[:, 0:2 * D].rearrange("p (m d) -> p m d", m=2)
                for t in range(NT):
                    link(v.tensor_scalar(xs[:, t, :], xs[:, t, :], mv[:, t, 0:1], small[:, 4 + t:5 + t], ALU.subtract, ALU.mult))
                    link(v.tensor_tensor(xs[:, t, :], xs[:, t, :], ln_bc[:, 0, :], ALU.mult))
                    ins = v.tensor_tensor(xs[:, t, :], xs[:, t, :], ln_bc[:, 1, :], ALU.add)
                    if t < NT - 1:
                        link(ins)
                ins.then_inc(norm_done, 1)

            def route(l):
                dve.wait_ge(er_ready, l + 1)
                sc, biased, gm, w = rt[:, 0], rt[:, 1], rt[:, 2], rt[:, 3]
                sigmoid_den(sc)
                for t in range(NT):
                    ins = v.tensor_tensor(biased[:, t, :], sc[:, t, :], rbias[:, l, :], ALU.add)
                link(ins)
                G = 8
                for t in range(NT):
                    for g in range(G):
                        ins = v.max(top8[:, t, g, :], biased[:, t, g * G:(g + 1) * G])
                link(ins)
                gs = gscore
                link(v.tensor_tensor(gs[:, 0], top8[:, :, :, 0], top8[:, :, :, 1], ALU.add))
                for t in range(NT):
                    ins = v.max(gs[:, 1, t, :], gs[:, 0, t, :])
                link(ins)
                link(v.memset(gs[:, 1, :, 4:8], -NEG))
                for t in range(NT):
                    ins = v.match_replace(gs[:, 2, t, :], gs[:, 1, t, :], gs[:, 0, t, :], NEG)
                link(ins)
                link(v.tensor_scalar(gs[:, 2], gs[:, 2], SELECTED, NEG, ALU.is_ge, ALU.mult))
                for g in range(G):
                    for t in range(NT):
                        ins = v.tensor_scalar(gm[:, t, g * G:(g + 1) * G], biased[:, t, g * G:(g + 1) * G],
                                              gs[:, 2, t, g:g + 1], None, ALU.add)
                link(ins)
                for t in range(NT):
                    ins = v.max(top8[:, t, 0, :], gm[:, t, :])
                link(ins)
                for t in range(NT):
                    ins = v.match_replace(w[:, t, :], top8[:, t, 0, :], gm[:, t, :], 2 * NEG)
                link(ins)
                sel = rt[:, 4]
                v.tensor_scalar(sel, w, 1.5 * NEG, None, ALU.is_lt).then_inc(chosen, 1)
                dve.wait_ge(chosen, l + 1)
                link(v.tensor_tensor(w, sel, sc, ALU.mult))
                link(v.tensor_reduce(gsum[:, 0, :], w, AX.X, ALU.add))
                link(v.reciprocal(gsum[:, 1, :], gsum[:, 0, :]))
                for t in range(NT):
                    ins = v.tensor_scalar(gates[:, t, :], w[:, t, :], gsum[:, 1, t:t + 1], 2.5, ALU.mult, ALU.mult)
                link(ins)

            def ffn_h(link, done):
                a = eh[:]
                sigmoid_den(a, link)
                link(v.tensor_tensor(a, a, pb[:, 0, :], ALU.mult))
                v.tensor_tensor(hT.rearrange("p k n -> p (k n)"), a, pb[:, 1, :], ALU.mult).then_inc(done, 1)

            def crowding(l):
                sel = rt[:, 4]
                dve.wait_ge(placed, l + 1)
                link(v.scalar_tensor_tensor(place[:], pb[:, 3, 0:2 * E].rearrange("p (t e) -> p t e", t=NT), 1.0, sel,
                                            ALU.add, ALU.mult))
                v.tensor_scalar(place[:], place[:], -1.0, None, ALU.add)
                link(v.tensor_reduce(gsum[:, 0, 0:1], pb[:, 3, 2 * E:3 * E], AX.X, ALU.max))
                v.tensor_scalar(flag[:], gsum[:, 0, 0:1], float(LIMIT), None, ALU.is_gt).then_inc(flag_ready, 1)
                dve.wait_ge(flag_ready, l + 1)

            def column(a, t, e):
                return a[:].rearrange("p t e -> p (t e)")[:, bass.ds(e + t * E, 1)]

            def all_tokens(l):
                link = Chain(dve, a_chain[l])
                for t, half in PARTS:
                    ins = v.tensor_copy(yacc[:, t, half * 512:(half + 1) * 512], pb[:, 4 + 2 * half + t, :])
                ins.then_inc(a_yacc[l], 1)
                K = 3
                with dve.Fori(0, E // 4) as i:
                    for e in range(4):
                        link.turn = i * (4 * K)
                        dve.wait_ge(a_exp[l], i * 4 + (e + 1))
                        ffn_h(link, a_h[l])
                        dve.wait_ge(a_down[l], i * 4 + (e + 1))
                        dve.wait_ge(a_yacc[l], i * 4 + (e + 1))
                        for t, half in PARTS:
                            a = yacc[:, t, half * 512:(half + 1) * 512]
                            ins = v.scalar_tensor_tensor(a, pb[:, 4 + 2 * half + t, :], column(gates, t, i * 4 + e), a,
                                                         ALU.mult, ALU.add)
                        ins.then_inc(a_yacc[l], 1)
                    assert link.n == 4 * K
                dve.wait_ge(a_yacc[l], E + 1)
                for t, half in PARTS:
                    o = slice(half * 512, half * 512 + 512)
                    ins = v.tensor_tensor(yacc[:, t, o], yacc[:, t, o], g_bc[:, 1, o], ALU.mult)
                ins.then_inc(yg_ready, 1)

            def compact(l):
                link = Chain(dve, c_chain[l])
                dve.wait_ge(utok_done[l], 1)
                v.tensor_copy(u_tok[:, 1].rearrange("p k c -> p (k c)"), pb[:, 2:4, :].rearrange("p b n -> p (b n)"))\
                    .then_inc(utok_ready[l], 1)

                def choice(e0, gathered):
                    if gathered is not None:
                        dve.wait_ge(xg_done[l], gathered)
                    for t in range(NT):
                        for e in range(2):
                            ins = v.tensor_scalar(choose[:, t, CAP * e:CAP * (e + 1)], slots[:], column(place, t, e0 + e), None,
                                                  ALU.is_equal)
                    ins.then_inc(choose_ready[l], 1)

                def weights(e0, read):
                    if read is not None:
                        dve.wait_ge(turned[l], read)
                    for t in range(NT):
                        for e in range(2):
                            ins = v.tensor_scalar(weigh[:, t, CAP * e:CAP * (e + 1)], slots[:], column(place, t, e0 + e),
                                                  column(gates, t, e0 + e), ALU.is_equal, ALU.mult)
                    ins.then_inc(weigh_ready[l], 1)

                def gathered(n):
                    dve.wait_ge(xg_done[l], n * 2)
                    v.tensor_copy(xg[:, 4:8, :].rearrange("p k s -> p (k s)"), pb[:, 1, :]).then_inc(xg1_ready[l], 1)

                def step(i, q, turn=0):
                    n, e0 = i * 2 + (q + 1), i * 4 + 2 * q
                    dve.wait_ge(sig_ready[l], n)
                    sigmoid_den(sig, link)
                    link(v.tensor_tensor(sig, sig, pb[:, 2, 0:F], ALU.mult))
                    v.tensor_tensor(h_tok, sig, pb[:, 2, F:2 * F], ALU.mult).then_inc(h_tok_ready[l], 1)
                    if turn < NP - 1:
                        gathered(n + 1)
                    if turn < NP - 2:
                        choice(e0 + 4, None)
                    if turn < NP - 1:
                        weights(e0 + 2, n)
                    dve.wait_ge(wd_free, i * 2 + (NP * l + q + 1))
                    v.tensor_copy(ysb[:, 512:1024], pb[:, 1, :]).then_inc(y1_read[l], 1)

                choice(0, None)
                weights(0, None)
                gathered(1)
                choice(2, 2)
                step(0, 0)
                n0 = link.n
                with dve.Fori(0, (NP - 4) // 2) as i:
                    link.turn = i * (2 * n0)
                    step(i, 1)
                    step(i, 2)
                assert link.n == 3 * n0
                link.turn, link.n = 0, n0 * (NP - 3)
                for p in range(NP - 3, NP):
                    step(p // 2, p % 2, turn=p)
                dve.wait_ge(scattered[l], 1)
                for t, half in PARTS:
                    o = slice(half * 512, half * 512 + 512)
                    ins = v.tensor_tensor(yacc[:, t, o], pb[:, 4 + 2 * half + t, :], g_bc[:, 1, o], ALU.mult)
                ins.then_inc(yg_ready, 1)

            for l in range(L):
                modulation(l)
                modulate(2 * l)
                for r in range(7):
                    rotary(l, r)
                indexer_keys(l)
                for r in range(7, NROPE):
                    rotary(l, r)
                indexer(l)
                for i in range(HC + 1):
                    if i < HC:
                        logits(l, i)
                    if i:
                        normalise(l, i - 1)
                merge(l)
                dve.wait_ge(y_done, 4 * (l + 1))
                norm(2 * l)
                modulate(2 * l + 1)
                route(l)
                dve.wait_ge(sh_exp, l + 1)
                ffn_h(link, sh_h)
                crowding(l)
                dve.wait_ge(sh_down, l + 1)
                crowded = dve.value_load(flag[0:1, 0:1], min_val=0, max_val=1)
                with dve.If(crowded > 0):
                    all_tokens(l)
                with dve.Else():
                    compact(l)
                dve.wait_ge(yg_ready, l + 1)
                norm(2 * l + 1, weighted=True)


def constants(S):
    import numpy as np
    P, NEG = 128, np.float32(-1.0e30)
    NT = S // P

    def rope_tables(dim):
        inv = np.float32(10000.0) ** (-np.arange(0, dim, 2, dtype=np.float32) / np.float32(dim))
        ang = np.arange(S, dtype=np.float32)[:, None] * inv[None, :].astype(np.float32)
        return np.cos(ang, dtype=np.float32), np.sin(ang, dtype=np.float32)

    rope = np.zeros((P, 4, S), np.float32)
    perm = np.zeros((P, 2, P), np.float32)
    for n, dim in enumerate((64, 32)):
        c, s = rope_tables(dim)
        h = dim // 2
        for p in range(P):
            rope[p, 2 * n], rope[p, 2 * n + 1] = c[:, p % h], s[:, p % h]
            if p % dim < h:
                perm[p + h, n, p] = -1.0
            else:
                perm[p - h, n, p] = 1.0
    c, s = rope_tables(32)
    ropei = np.stack([c.reshape(NT, P, 16), s.reshape(NT, P, 16)]).transpose(2, 0, 1, 3)
    masks = np.full((P, 2, P + S), NEG, np.float32)
    for t, off in ((0, 0), (1, P)):
        q = (t * P + np.arange(P))[:, None]
        k = np.arange(P * (t + 1))[None, :]
        d = q - k
        masks[:, 0, off:off + P * (t + 1)] = np.where(d >= 0, np.float32(0), NEG)
        count = np.zeros(d.shape, np.int64)
        for window, dil in ((128, 1), (512, 4), (2048, 16)):
            count += (d >= 0) & (d <= window) & (d % dil == 0)
        masks[:, 1, off:off + P * (t + 1)] = np.where(count > 0, np.log(np.maximum(count, 1)), NEG)
    return {"ident": np.eye(P, dtype=np.float32), "perm": perm, "rope": rope,
            "ropei_tok": np.ascontiguousarray(ropei), "masks": masks,
            "before": np.triu(np.ones((P, P), np.float32), 1),
            "slots": np.tile(np.arange(64, dtype=np.float32), (P, 1))}


def kernel(**inputs):
    import numpy as _np
    import concourse.bacc as _bacc
    from concourse import mybir as _mybir
    from concourse.bass_utils import run_bass_kernel_spmd as _run

    g = {n: _np.asarray(a) for n, a in inputs.items()}
    L, D, KD = g["w_in"].shape[0], g["w_in"].shape[1], 8
    c = constants(g["x"].shape[1])
    ada_b = g["ada_b"].reshape(L, 6, 128, KD)
    arrays = {
        "x": g["x"][0], "cT": g["c"].reshape(128, KD), "ada_w": g["ada_w"],
        "adaT_b": _np.ascontiguousarray(ada_b[:, (0, 1, 3, 4)].transpose(2, 0, 1, 3)), "ada_b": g["ada_b"],
        "w_in": g["w_in"], "ik_gb": _np.stack([g["ik_norm_g"], g["ik_norm_b"]], 1),
        "w_br_a": g["w_br_a"], "w_br_b": g["w_br_b"], "w_br_c": g["w_br_c"], "w_out": g["w_out"],
        "ln_gb": _np.stack([_np.stack([g["ln1_g"], g["ln1_b"]], 1), _np.stack([g["ln2_g"], g["ln2_b"]], 1)], 1),
        "w_router": g["w_router"], "router_bias": g["router_bias"],
        "w_gate": g["w_gate"], "w_up": g["w_up"], "w_down": g["w_down"],
        "ws_gate": g["ws_gate"], "ws_up": g["ws_up"], "ws_down": g["ws_down"],
        "ident_c": c["ident"], "perm_c": c["perm"], "rope_c": c["rope"], "ropei_tok_c": c["ropei_tok"], "mask_c": c["masks"],
        "before_c": c["before"], "slot_c": c["slots"],
    }
    nc = _bacc.Bacc("TRN2", target_bir_lowering=False, num_devices=1)
    given, args = {}, []
    for name, a in arrays.items():
        a = _np.ascontiguousarray(a)
        given[f"in_{name}"] = a
        args.append(nc.dram_tensor(f"in_{name}", a.shape, _mybir.dt.from_np(a.dtype), kind="ExternalInput").ap())
    args.append(nc.dram_tensor("out_0", g["x"].shape[1:], F32, kind="ExternalOutput").ap())
    build(nc, *args)
    r = _run(nc, [given], core_ids=[0])
    return r.results[0]["out_0"][None]
```

```python
from contextlib import ExitStack

import concourse.bass as bass
from concourse import mybir

F32 = mybir.dt.float32
F32R = mybir.dt.float32r
ALU = mybir.AluOpType
ACT = mybir.ActivationFunctionType
AX = mybir.AxisListType

P = 128
NEG = -1.0e30
SELECTED = -5.0e29
LIMIT = 64


def build(nc, x, cT, ada_w, adaT_b, ada_b, w_in, ik_gb, w_br_a, w_br_b, w_br_c, w_out, ln_gb,
          w_router, router_bias, w_gate, w_up, w_down, ws_gate, ws_up, ws_down,
          ident_c, perm_c, rope_c, ropei_tok_c, mask_c, lnT_c, before_c, slot_c, out):
    L, D, WIN = w_in.shape
    S = x.shape[0]
    E, F = w_gate.shape[1], w_gate.shape[3]
    DH, IH, ID = 64, 8, 32
    KD = D // P
    KF = F // P
    NT = S // P
    SC = 512
    HC = 3 * 8
    TOPK_ROUNDS = 64 // 8
    ALPHA = float((2 * L) ** 0.25)
    EPS = 1e-5
    SCALE = float(DH) ** -0.5
    KEYS = [P * (t + 1) for t in range(NT)]
    KOFF = [0, P]
    KALL = sum(KEYS)

    A_Q, A_SMALL, B_Q, B_K, B_V, C_Q, C_K, C_V, G_A = 0, 512, 936, 1448, 1960, 2472, 2984, 3496, 4008
    SMALL = B_Q - A_SMALL
    assert WIN == G_A + 3 * D and D == 1024 and NT == 2 and F == 256

    GROUPS = ("qa", "small", "qb", "kb", "vb", "qc", "kc", "vc")
    BLOCKS = (4, 3, 4, 4, 0, 4, 4, 0)
    NEXT_ADA = {"qa": 0, "kb": 1, "qc": 2, "kc": 3}
    OWN_ADA = (4, 6, 5, 7, 10, 8, 11, 9)
    EVERY = 3 * KD // len(OWN_ADA)
    ada_with = [[[(l + 1, NEXT_ADA[n])] if n in NEXT_ADA and l + 1 < L else [] for n in GROUPS] for l in range(L)]
    own_ada = [[(l, j) for j in OWN_ADA] for l in range(L)]
    ada_order = [(0, j) for j in range(4)] + [a for l in range(L) for g in ada_with[l] + [own_ada[l]] for a in g]
    items = [(0, "ada", j) for j in range(4)]
    for l in range(L):
        for n, name in enumerate(GROUPS):
            items.append((l, name, 0))
        for n in range(6):
            items += [(l, "gate", n), (l, "br", n)]
        items += [(l, "wout", 0), (l, "ln", 0), (l, "router", 0), (l, "sh_gu", 0), (l, "sh_d", 0),
                  (l, "ln", 1), (l, "expert", E - 2), (l, "scratch", 0)]
    UNITS, UNIT = 6, KD * F
    N_UNITS = {"br": 1, "ln": 1, "router": 1, "sh_d": 1, "scratch": 1, "expert": 3}
    N_DMAS = {"sh_gu": 2, "ln": 2, "scratch": 0, "expert": 3}
    start, landed, before_in = {}, {}, {}
    owner, count, pos = [None] * UNITS, [0] * UNITS, 0
    for it in items:
        size = N_UNITS.get(it[1], 2)
        pos = {("gate", 0): 0, ("ln", 1): 4, ("expert", E - 2): 1, ("scratch", 0): 5}\
            .get(it[1:], pos if pos + size <= UNITS else 0)
        start[it] = pos
        before_in[it] = {owner[u] for u in range(pos, pos + size)} - {None}
        for u in range(pos, pos + size):
            owner[u] = it
        count[pos] += 16 * N_DMAS.get(it[1], 1)
        landed[it] = count[pos]
        pos = (pos + size) % UNITS
    WIN_AT = {"qa": A_Q, "small": A_SMALL, "qb": B_Q, "kb": B_K, "vb": B_V, "qc": C_Q, "kc": C_K, "vc": C_V}

    NROPE, NTOK, NIDX, NGB = 23, 6, NT * IH, 3 * KD
    CAP = 64
    NP = E // 2

    with ExitStack() as ctx:
        def sb(name, shape, dt=F32):
            return ctx.enter_context(nc.sbuf_tensor(name, shape, dt))

        def sem(name):
            return ctx.enter_context(nc.semaphore(name))

        pb = ctx.enter_context(nc.psum_tensor("pb", [P, 8, 512], F32))

        ring = sb("ring", [P, UNITS * UNIT])
        experts = sb("experts", [P, 2, 2, 3, KD * F])
        xs = sb("xs", [P, NT, D])
        with ExitStack() as shared:
            def fp32(name, shape):
                return shared.enter_context(nc.sbuf_tensor(name, shape, F32))

            uT = fp32("uT", [P, KD, S])
            acc = fp32("acc", [P, 2, SC])
            yacc = fp32("yacc", [P, NT, D])
            hbuf = fp32("hbuf", [P, 4 * S])
            eh = fp32("eh", [P, KF * S])
            sg = fp32("sg", [P, 2, S])
        u_half = sb("u_half", [P, NT, 2, KD, P], F32R)
        y_half = sb("y_half", [P, 2, D], F32R)
        choose = sb("choose", [P, NT, P], F32R)
        unchoose = sb("unchoose", [P, 2, S], F32R)
        weigh = sb("weigh", [P, NT, P])
        ident = sb("ident", [P, P])
        perm = sb("perm", [P, 2, P])
        rope = sb("rope", [P, 4, S])
        ropei_tok = sb("ropei_tok", [P, 2, NT, ID // 2])
        masks = sb("masks", [P, 3, KALL])
        CAUSAL, DILATED, INDEXED = 0, 1, 2
        ones = sb("ones", [P, P])
        g_bc = sb("g_bc", [P, 2, D])
        modT = sb("modT", [P, L, 4, KD])
        adaT_bias = sb("adaT_bias", [P, L, 4, KD])
        ikgb = sb("ikgb", [P, L, 2, ID])
        rbias = sb("rbias", [P, L, E])
        lnT = sb("lnT", [P, L, 2, 2, KD])
        turnT = sb("turnT", [P, 2, KD])
        silu_c = sb("silu_c", [P, 3, KD])
        small = sb("small", [P, 64])
        stats = sb("stats", [P, 4, 6])
        negmax = sb("negmax", [P, 4, NT])
        esum = sb("esum", [P, 4, NT])
        rden = sb("rden", [P, 4, NT])
        gates = sb("gates", [P, NT, E])
        rt = sb("rt", [P, 5, NT, E])
        top8 = sb("top8", [P, NT, 8, 8])
        gate_of = sb("gate_of", [P, 1])
        before = sb("before", [P, P])
        slots = sb("slots", [P, CAP])
        place = sb("place", [P, NT, E])
        flag = sb("flag", [P, 1], mybir.dt.int32)
        powc = sb("powc", [P, 2])

        lend = experts[:, 1].rearrange("p e m n -> p (e m n)")
        at = [0]

        def part(*shape):
            n = 1
            for s in shape:
                n *= s
            a = lend[:, at[0]:at[0] + n]
            at[0] += n
            assert at[0] <= 2 * 3 * KD * F
            names = "abc"[:len(shape)]
            if len(shape) == 1:
                return a
            return a.rearrange(f"p ({' '.join(names)}) -> p {' '.join(names)}",
                               **{c: s for c, s in zip(names, shape)})

        qT = [part(4, S) for _ in range(3)]
        kT = [part(1, S), part(4, S), part(4, S)]
        v_a = part(NT, DH)
        v_b = part(NT, 512)
        v_c = part(NT, 512)
        oT = [part(4, S) for _ in range(3)]
        qiT = part(2, S)
        kiT = part(S)
        mergedT = lend[:, 0:KD * S].rearrange("p (k n) -> p k n", k=KD)
        score = hbuf[:, 0:KALL]
        relu = sg
        ki_tok = rt[:].rearrange("p a t e -> p (a t e)")
        lg = yacc[:].rearrange("p t d -> p (t d)")[:, 0:4 * KALL].rearrange("p (a n) -> p a n", a=4)
        pT = part(2, KALL)
        raw = eh[:].rearrange("p (a n) -> p a n", a=2)
        ropetmp = hbuf[:, 512:1024].rearrange("p (a n) -> p a n", a=2)
        hT = hbuf[:, 0:KF * S].rearrange("p (k n) -> p k n", k=KF)

        ki_rows = sb("ki_rows", [P, NT, ID + IH])
        ki_tmp = sb("ki_tmp", [P, NT, ID])
        ki_prod = sb("ki_prod", [P, 4, NT, ID // 2])
        mark = sb("mark", [P, 1])
        wi = sb("wi", [P, NT, IH])
        mv = sb("mv", [P, NT, 2])
        ve = small[:, 2:4]
        rs = small[:, 4:6]
        gscore = sb("gscore", [P, 3, NT, 8])
        gsum = sb("gsum", [P, 2, NT])

        FIRST_LOADS = [(ident[:], ident_c), (adaT_bias[:], adaT_b), (xs[:], x.rearrange("(t p) d -> p t d", p=P))]
        SCORE_BANK = (0, 1, 6)
        UTOK_BANK = (4, 2)
        CONST_LOADS = [
            (perm[:], perm_c), (lnT[:], lnT_c),
            (rope[:], rope_c), (ropei_tok[:], ropei_tok_c), (masks[:, 0:2, :], mask_c),
            (before[:], before_c), (slots[:], slot_c),
            (ikgb[:].rearrange("p l a i -> p (l a i)"), ik_gb.rearrange("l a i -> (l a i)").partition_broadcast(P)),
            (rbias[:].rearrange("p l e -> p (l e)"), router_bias.rearrange("l e -> (l e)").partition_broadcast(P)),
        ]

        first_landed = sem("first_landed")
        consts_landed = sem("consts_landed")
        c_landed = sem("c_landed")
        ring_landed = [sem(f"ring_landed{u}") for u in range(UNITS)]
        gu_landed = [sem(f"gu_landed{i}") for i in range(2)]
        wd_landed = [sem(f"wd_landed{i}") for i in range(2)]
        gu_free = sem("gu_free")
        wd_free = sem("wd_free")
        gbias_landed = sem("gbias_landed")
        lent_landed = [sem(f"lent_landed{i}") for i in range(3)]
        silu_exp = sem("silu_exp")
        ones_ready = sem("ones_ready")
        acc_ready = sem("acc_ready")
        mod_done = sem("mod_done")
        mod_read = sem("mod_read")
        xT_done = sem("xT_done")
        uT_lo = sem("uT_lo")
        uT_hi = sem("uT_hi")
        turnT_ready = sem("turnT_ready")
        xn_ready = sem("xn_ready")
        den_ready = sem("den_ready")
        proj_done = sem("proj_done")
        raw_ready = sem("raw_ready")
        perm_done = sem("perm_done")
        rope_done = sem("rope_done")
        tok_done = sem("tok_done")
        tok_read = sem("tok_read")
        ki_ready = sem("ki_ready")
        kiT_done = sem("kiT_done")
        kiT_ready = sem("kiT_ready")
        idx_done = sem("idx_done")
        relu_ready = sem("relu_ready")
        score_used = sem("score_used")
        s_done = sem("s_done")
        s_read = sem("s_read")
        max_ready = sem("max_ready")
        exp_done = sem("exp_done")
        p_ready = sem("p_ready")
        pt_done = sem("pt_done")
        pt_ready = sem("pt_ready")
        pv_done = sem("pv_done")
        o_read = sem("o_read")
        gb_done = sem("gb_done")
        eg_ready = sem("eg_ready")
        merged_done = sem("merged_done")
        y_done = sem("y_done")
        var_ready = sem("var_ready")
        rstd_ready = sem("rstd_ready")
        norm_done = sem("norm_done")
        first_tile_done = sem("first_tile_done")
        router_done = sem("router_done")
        er_ready = sem("er_ready")
        sh_gate_done = sem("sh_gate_done")
        sh_gu_done = sem("sh_gu_done")
        sh_sig = sem("sh_sig")
        sh_h = sem("sh_h")
        sh_down = sem("sh_down")
        chosen = sem("chosen")
        placed = sem("placed")
        flag_ready = sem("flag_ready")

        def per_layer(name):
            return [sem(f"{name}{l}") for l in range(L)]

        a_gu, a_exp, a_h, a_down, a_yacc, a_chain = (per_layer(n) for n in (
            "all_gu", "all_exp", "all_h", "all_down", "all_yacc", "all_chain"))
        utok_done, utok_ready = per_layer("utok_done"), per_layer("utok_ready")
        utok_hi = per_layer("utok_hi")
        choose_ready, weigh_ready = per_layer("choose_ready"), per_layer("weigh_ready")
        xg_done, xg0_ready, xg1_ready = per_layer("xg_done"), per_layer("xg0_ready"), per_layer("xg1_ready")
        sig_ready, h_tok_ready = per_layer("sig_ready"), per_layer("h_tok_ready")
        turned, hgT_ready, unchoose_ready = per_layer("turned"), per_layer("hgT_ready"), per_layer("unchoose_ready")
        y0_done, y_hi, y_ready = per_layer("y0_done"), per_layer("y_hi"), per_layer("y_ready")
        scattered, c_chain = per_layer("scattered"), per_layer("compact_chain")
        yg_ready = sem("yg_ready")
        dve_chain = sem("dve_chain")
        pool_chain = sem("pool_chain")
        out_stored = sem("out_stored")

        class Chain:

            def __init__(self, eng, s):
                self.eng, self.s, self.n, self.turn = eng, s, 0, 0

            def __call__(self, ins):
                ins.then_inc(self.s, 1)
                self.n += 1
                self.eng.wait_ge(self.s, self.turn + self.n)

        def ring_ap(l, item):
            o = start[(l,) + item] * UNIT
            return ring[:, o:o + UNIT * N_UNITS.get(item[0], 2)]

        lent = [a for l in range(L) for a in sum(ada_with[l], []) + own_ada[l] + [(l, "wout")]]

        def lent_buffer(l, j):
            n = lent.index((l, j))
            a = experts[:, 0].rearrange("p e m n -> p (e m n)")[:, (n % 3) * KD * SC:(n % 3 + 1) * KD * SC]
            return a.rearrange("p (k c) -> p k c", k=KD), lent_landed[n % 3], 16 * (n // 3 + 1)

        def wait_item(eng, l, item):
            eng.wait_ge(ring_landed[start[(l,) + item]], landed[(l,) + item])

        def scratch(l):
            a = ring_ap(l, ("scratch", 0))
            return (a[:, 0:D].rearrange("p (k s) -> p k s", k=KD),
                    a[:, D:D + F],
                    a[:, D + F:D + 2 * F],
                    a[:, D + 2 * F:D + 3 * F].rearrange("p (k s) -> p k s", k=KF),
                    weigh)

        block = ctx.enter_context(nc.Block())

        @block.sync
        def _(sp):
            def used(item):
                l, kind, j = item
                rope_at = {"qa": 4, "qb": 11, "kb": 15, "qc": 19, "kc": 23}
                tok_at = {"small": 2, "vb": 4, "vc": 6}
                if kind == "ada":
                    sp.wait_ge(acc_ready, ada_order.index((l, j)) + 1)
                elif kind in rope_at:
                    sp.wait_ge(proj_done, NROPE * l + rope_at[kind])
                elif kind in tok_at:
                    sp.wait_ge(tok_done, NTOK * l + tok_at[kind])
                elif kind in ("gate", "br"):
                    sp.wait_ge(gb_done, NGB * l + 4 * (j + 1))
                elif kind == "wout":
                    sp.wait_ge(y_done, 4 * l + 3)
                elif kind == "ln":
                    sp.wait_ge(norm_done, 2 * l + j + 1)
                elif kind == "sh_gu":
                    sp.wait_ge(sh_gu_done, l + 1)
                elif kind == "router":
                    sp.wait_ge(router_done, l + 1)
                elif kind == "sh_d":
                    sp.wait_ge(sh_down, l + 1)
                elif kind == "expert":
                    sp.wait_ge(wd_free, NP * (l + 1))
                else:
                    sp.wait_ge(norm_done, 2 * l + 2)

            def load_item(item):
                l, kind, j = item
                for it in sorted(before_in[item], key=items.index):
                    used(it)
                dst, s = ring_ap(l, (kind, j)), ring_landed[start[item]]
                if kind == "ada":
                    sp.dma_start(dst.rearrange("p (k c) -> p k c", k=KD),
                                 ada_w[l, :, j * SC:(j + 1) * SC].rearrange("(p k) c -> p k c", k=KD)).then_inc(s, 16)
                elif kind in WIN_AT or kind == "gate":
                    c0 = WIN_AT[kind] if kind in WIN_AT else G_A + j * SC
                    w = SMALL if kind == "small" else SC
                    sp.dma_start(dst.rearrange("p (k c) -> p k c", k=KD)[:, :, 0:w],
                                 w_in[l, :, c0:c0 + w].rearrange("(p k) c -> p k c", k=KD)).then_inc(s, 16)
                elif kind == "br":
                    w, c0 = (w_br_a, w_br_b, w_br_c)[j // 2], (j % 2) * SC
                    sp.dma_start(dst.rearrange("p (b c) -> p b c", b=4),
                                 w[l, :, c0:c0 + SC].rearrange("(b p) c -> p b c", p=P)).then_inc(s, 16)
                elif kind == "wout":
                    sp.dma_start(dst.rearrange("p (k c) -> p k c", k=KD),
                                 w_out[l, :, j * SC:(j + 1) * SC].rearrange("(k p) c -> p k c", p=P)).then_inc(s, 16)
                elif kind == "ln":
                    for m in range(2):
                        sp.dma_start(dst[:, m * D:(m + 1) * D], ln_gb[l, j, m].partition_broadcast(P)).then_inc(s, 16)
                elif kind == "sh_gu":
                    for m, w in enumerate((ws_gate, ws_up)):
                        sp.dma_start(dst[:, m * UNIT:(m + 1) * UNIT], w[l].rearrange("(p k) c -> p (k c)", k=KD)).then_inc(s, 16)
                elif kind == "sh_d":
                    sp.dma_start(dst, ws_down[l].rearrange("(p k) c -> p (k c)", k=KF)).then_inc(s, 16)
                elif kind == "expert":
                    for m, (w, k) in enumerate(((w_gate, KD), (w_up, KD), (w_down, KF))):
                        sp.dma_start(dst[:, m * UNIT:(m + 1) * UNIT], w[l, j].rearrange("(p k) c -> p (k c)", k=k)).then_inc(s, 16)
                else:
                    sp.dma_start(dst[:, 0:KD * E], w_router[l].rearrange("(p k) c -> p (k c)", k=KD)).then_inc(s, 16)

            def load_pair(l, slot, e0, used=None, n=2):
                if used is not None:
                    sp.wait_ge(gu_free, used)
                mine = slice(2 - n, 2)
                for m, w in enumerate((w_gate, w_up)):
                    sp.dma_start(experts[:, slot, mine, m, :],
                                 w[l, bass.ds(e0 + 2 - n, n)].rearrange("e (p k) c -> p e (k c)", k=KD))\
                        .then_inc(gu_landed[slot], 16)
                if used is not None:
                    sp.wait_ge(wd_free, used)
                sp.dma_start(experts[:, slot, mine, 2, :],
                             w_down[l, bass.ds(e0 + 2 - n, n)].rearrange("e (p k) c -> p e (k c)", k=KF))\
                    .then_inc(wd_landed[slot], 16)

            sp.dma_start(silu_c[:, 0, :], cT).then_inc(c_landed, 16)
            at = 0
            for l in range(L):
                end = items.index((l, "ln", 1))
                while at < end:
                    load_item(items[at])
                    at += 1
                sp.wait_ge(y_done, 4 * (l + 1))
                load_pair(l, 0, 0)
                load_pair(l, 1, 2)
                load_item(items[at])
                load_item(items[at + 1])
                at += 3
                with sp.Fori(1, NP // 2 - 1) as i:
                    for slot in range(2):
                        load_pair(l, slot, i * 4 + 2 * slot, i * 2 + (NP * l + slot - 1))
                load_pair(l, 0, E - 4, NP * (l + 1) - 3)
                load_pair(l, 1, E - 2, NP * (l + 1) - 2, n=1)
            for t, done in ((0, first_tile_done), (1, norm_done)):
                sp.wait_ge(done, 1 if t == 0 else 2 * L)
                sp.dma_start(out[t * P:(t + 1) * P, :], xs[:, t, :]).then_inc(out_stored, 16)
            sp.wait_ge(out_stored, 16 * NT)

        @block.gpsimd
        def _(pool):
            nc.gpsimd.memset(powc[:], -0.5).then_inc(pool_chain, 1)
            pool.wait_ge(pool_chain, 1)

            def rstd(n, t):
                o = slice(t, t + 1) if t is not None else slice(0, NT)
                pool.wait_ge(var_ready, n)
                nc.gpsimd.tensor_tensor(rs[:, o], ve[:, o], powc[:, o], ALU.pow).then_inc(rstd_ready, 1)

            for l in range(L):
                if l:
                    pool.wait_ge(norm_done, 2 * l)
                else:
                    pool.wait_ge(acc_ready, 4)
                for m, piece in enumerate((2, 5)):
                    pool.dma_start(g_bc[:, m, :], ada_b[l, piece * D:(piece + 1) * D].partition_broadcast(P))\
                        .then_inc(gbias_landed, 16)
                rstd(5 * l + 1, None)
                for i in range(HC):
                    pool.wait_ge(den_ready, HC * l + i + 1)
                    for t in range(NT):
                        a = lg[:, i % 4, KOFF[t]:KOFF[t] + KEYS[t]]
                        ins = nc.gpsimd.tensor_scalar(a, a, rden[:, i % 4, t:t + 1], 1.0, ALU.mult, ALU.mult)
                    ins.then_inc(p_ready, 1)
                for n in range(4):
                    rstd(5 * l + 2 + n, n % 2)
                    if l == L - 1 and n == 2:
                        wait_item(pool, l, ("ln", 1))
                        ln_bc = ring_ap(l, ("ln", 1)).rearrange("p (m d) -> p m d", m=2)
            pool.wait_ge(xn_ready, 4 * L - 1)
            nc.gpsimd.tensor_tensor(xs[:, 0, :], xs[:, 0, :], ln_bc[:, 0, :], ALU.mult).then_inc(pool_chain, 1)
            pool.wait_ge(pool_chain, 2)
            nc.gpsimd.tensor_tensor(xs[:, 0, :], xs[:, 0, :], ln_bc[:, 1, :], ALU.add).then_inc(first_tile_done, 1)

        @block.tensor
        def _(pe):
            mm = nc.tensor.matmul

            def transpose_x(n):
                for t in range(NT):
                    if n:
                        pe.wait_ge(xn_ready, 2 * (n - 1) + t + 1)
                    for k in range(KD):
                        o = (k % 2) * S + t * P
                        ins = nc.tensor.transpose(pb[:, k // 2, o:o + P], xs[:, t, k::KD], ident[:])
                        if k % 2 and t == NT - 1:
                            ins.then_inc(xT_done, 1)

            def contract(dst, lhs, rhs, n):
                for k in range(n):
                    ins = mm(dst, lhs(k), rhs(k), start=(k == 0), stop=(k == n - 1))
                return ins

            def modulation(l, j):
                a = ada_order.index((l, j))
                pe.wait_ge(acc_ready, a + 1)
                if j // 2 in (2, 5):
                    ins = mm(pb[:, 6, :], ones[:], acc[:, a % 2, :], start=True, stop=True)
                else:
                    q = (0, 1, None, 2, 3)[j // 2]
                    h = 64 * (j % 2)
                    for k in range(KD):
                        ins = mm(pb[h:h + 64, 7, q * KD + k:q * KD + k + 1], acc[:, a % 2, k::KD], ones[:, 0:1],
                                 start=True, stop=True)
                ins.then_inc(mod_done, 1)

            def rotate_half(r, l):
                pe.wait_ge(raw_ready, NROPE * l + r + 1)
                if r >= 2:
                    pe.wait_ge(rope_done, NROPE * l + r - 1)
                mm(pb[:, 2 + r % 2, 0:S], perm[:, 1 if r in (5, 6) else 0, :], raw[:, r % 2, :], start=True, stop=True)\
                    .then_inc(perm_done, 1)

            def projections(l):
                mods = []
                r = turned_upto = 0
                for n, (name, blocks) in enumerate(zip(GROUPS, BLOCKS)):
                    wait_item(pe, l, (name, 0))
                    w = ring_ap(l, (name, 0)).rearrange("p (k c) -> p k c", k=KD)
                    for b in range(blocks):
                        if r >= 2:
                            pe.wait_ge(raw_ready, NROPE * l + r - 1)
                        if name == "small" and b == 0:
                            for h in range(2):
                                ins = contract(pb[64 * h:64 * h + 64, r % 2, 0:S], lambda k: w[:, k, 0:DH],
                                               lambda k: uT[:, k, :], KD)
                        else:
                            c0 = b * P if name != "small" else 2 * DH + (b - 1) * P
                            ins = contract(pb[:, r % 2, 0:S], lambda k: w[:, k, c0:c0 + P], lambda k: uT[:, k, :], KD)
                        ins.then_inc(proj_done, 1)
                        if turned_upto < r:
                            rotate_half(r - 1, l)
                            turned_upto = r
                        r += 1
                        if mods and b == 1:
                            modulation(*mods.pop())
                    if name in ("small", "vb", "vc"):
                        g = ("small", "vb", "vc").index(name)
                        for t in range(NT):
                            if g:
                                pe.wait_ge(tok_read, NTOK * l + 2 * (g - 1) + t + 1)
                                pe.wait_ge(relu_ready, NIDX * (l + 1))
                            lhs = lambda k: uT[:, k, t * P:(t + 1) * P]
                            if g == 0:
                                contract(pb[:, 4 + t, 0:DH], lhs, lambda k: w[:, k, DH:2 * DH], KD)
                                ins = contract(pb[:, 4 + t, DH:DH + ID + IH], lhs, lambda k: w[:, k, 384:384 + ID + IH], KD)
                            else:
                                ins = contract(pb[:, 4 + t, :], lhs, lambda k: w[:, k, :], KD)
                            ins.then_inc(tok_done, 1)
                            if turned_upto < r:
                                rotate_half(r - 1, l)
                                turned_upto = r
                            if mods and g and t == 0:
                                modulation(*mods.pop())
                    mods += ada_with[l][n]
                    if name == "qb":
                        rotate_half(r - 1, l)
                        turned_upto = r
                        indexer(l)

            def indexer(l):
                pe.wait_ge(ki_ready, l + 1)
                for t in range(NT):
                    ins = nc.tensor.transpose(pb[:, 7, S + t * P:S + (t + 1) * P], ki_tok[:, t * P:(t + 1) * P], ident[:])
                ins.then_inc(kiT_done, 1)
                pe.wait_ge(kiT_ready, l + 1)
                pe.wait_ge(rope_done, NROPE * l + 7)
                pe.wait_ge(tok_read, NTOK * l + 2)
                i = 0
                for t in range(NT):
                    for h in range(IH):
                        if i >= 2:
                            pe.wait_ge(relu_ready, NIDX * l + i - 1)
                        r = ID * (h % 4)
                        mm(pb[:, 4 + i % 2, 0:KEYS[t]], qiT[r:r + ID, h // 4, t * P:(t + 1) * P], kiT[r:r + ID, 0:KEYS[t]],
                           start=True, stop=True, tile_position=(r, 0)).then_inc(idx_done, 1)
                        i += 1

            ORDER = [(br, h) for br in (1, 2, 0) for h in range(8)]

            def scores(l, i):
                br, h = ORDER[i]
                r = DH * (h % 2)
                if i >= 3:
                    pe.wait_ge(s_read, HC * l + i - 2)
                for t in range(NT):
                    ins = mm(pb[:, SCORE_BANK[i % 3], KOFF[t]:KOFF[t] + KEYS[t]], qT[br][r:r + DH, h // 2, t * P:(t + 1) * P],
                             kT[br][r:r + DH, (h // 2 if br else 0), 0:KEYS[t]], start=True, stop=True)
                ins.then_inc(s_done, 1)

            def turn_probs(l, i):
                pe.wait_ge(p_ready, HC * l + i + 1)
                if i >= 2:
                    pe.wait_ge(pt_ready, HC * l + i - 1)
                for m in range(3):
                    ins = nc.tensor.transpose(pb[:, 2 + i % 2, m * P:(m + 1) * P], lg[:, i % 4, m * P:(m + 1) * P], ident[:])
                ins.then_inc(pt_done, 1)

            def values(l, i):
                br, h = ORDER[i]
                hp = i // 2
                pe.wait_ge(pt_ready, HC * l + i + 1)
                if i % 2 == 0 and hp >= 2:
                    pe.wait_ge(o_read, HC // 2 * l + hp - 1)
                v = (v_a, v_b, v_c)[br]
                c = 0 if br == 0 else h * DH
                o = pb[DH * (h % 2):DH * (h % 2) + DH, 4 + hp % 2, 0:S]
                mm(o, v[:, 0, c:c + DH], pT[:, i % 2, 0:S], start=True, stop=False)
                mm(o[:, P:S], v[:, 1, c:c + DH], pT[:, i % 2, S:S + P], start=False, stop=True).then_inc(pv_done, 1)

            def attention(l):
                pe.wait_ge(tok_read, NTOK * (l + 1))
                pe.wait_ge(rope_done, NROPE * (l + 1))
                for i in range(HC + 4):
                    if i < HC:
                        scores(l, i)
                    if 3 <= i < HC + 3:
                        turn_probs(l, i - 3)
                    if 4 <= i:
                        values(l, i - 4)

            def branches(l):
                pe.wait_ge(o_read, HC // 2 * (l + 1))
                for j in range(NGB):
                    br, k, n = j // KD, j % KD, j // 4
                    if j % 4 == 0:
                        wait_item(pe, l, ("gate", n))
                        wait_item(pe, l, ("br", n))
                        wg = ring_ap(l, ("gate", n)).rearrange("p (k c) -> p k c", k=KD)
                        wb = ring_ap(l, ("br", n)).rearrange("p (b c) -> p b c", b=4)
                    if j >= 2:
                        pe.wait_ge(merged_done, NGB * l + j - 1)
                    c = slice((k % 4) * P, (k % 4 + 1) * P)
                    contract(pb[:, 2 + j % 2, 0:S], lambda b: wb[:, b, c], lambda b: oT[br][:, b, :], 4)
                    contract(pb[:, j % 2, 0:S], lambda q: wg[:, q, c], lambda q: uT[:, q, :], KD).then_inc(gb_done, 1)
                    if j >= EVERY + 1 and (j - EVERY - 1) % EVERY == 0:
                        modulation(*own_ada[l][(j - EVERY - 1) // EVERY])
                modulation(*own_ada[l][-1])

            def mix_out(l):
                pe.wait_ge(merged_done, NGB * (l + 1))
                pe.wait_ge(mod_read, ada_order.index(own_ada[l][-1]) + 1)
                wait_item(pe, l, ("wout", 0))
                left = ring_ap(l, ("wout", 0)).rearrange("p (k c) -> p k c", k=KD)
                right, landed_sem, value = lent_buffer(l, "wout")
                for t in range(NT):
                    for half, w in enumerate((left, right)):
                        if half and t == 0:
                            pe.wait_ge(landed_sem, value)
                        contract(pb[:, 4 + 2 * half + t, :], lambda k: mergedT[:, k, t * P:(t + 1) * P],
                                 lambda k: w[:, k, :], KD).then_inc(y_done, 1)

            def router(l):
                wait_item(pe, l, ("router", 0))
                w = ring_ap(l, ("router", 0))[:, 0:KD * E].rearrange("p (k c) -> p k c", k=KD)
                pe.wait_ge(uT_lo, 2 * l + 2)
                pe.wait_ge(uT_hi, 2 * l + 2)
                for t in range(NT):
                    ins = contract(pb[:, 2, t * E:(t + 1) * E], lambda k: uT[:, k, t * P:(t + 1) * P], lambda k: w[:, k, :], KD)
                ins.then_inc(router_done, 1)
                pe.wait_ge(er_ready, l + 1)

            def gate_or_up(q, w):
                for m in range(KF):
                    ins = contract(pb[:, q, m * S:(m + 1) * S], lambda k: w[:, k, m::KF], lambda k: uT[:, k, :], KD)
                return ins

            def down(wd, done):
                for t in range(NT):
                    for half in range(2):
                        ins = contract(pb[:, 4 + 2 * half + t, :], lambda k: hT[:, k, t * P:(t + 1) * P],
                                       lambda k: wd[:, k, half * 512:(half + 1) * 512], KF)
                ins.then_inc(done, 1)

            def places(l):
                sel = rt[:, 4]
                pe.wait_ge(chosen, l + 1)
                mm(pb[:, 3, 0:E], before[:], sel[:, 0, :], start=True, stop=True)
                mm(pb[:, 3, E:2 * E], before[:], sel[:, 1, :], start=True, stop=False)
                mm(pb[:, 3, E:2 * E], ones[:], sel[:, 0, :], start=False, stop=True)
                mm(pb[:, 3, 2 * E:3 * E], ones[:], sel[:, 0, :], start=True, stop=False)
                mm(pb[:, 3, 2 * E:3 * E], ones[:], sel[:, 1, :], start=False, stop=True).then_inc(placed, 1)

            def shared_down(l):
                pe.wait_ge(sh_h, l + 1)
                wait_item(pe, l, ("sh_d", 0))
                down(ring_ap(l, ("sh_d", 0)).rearrange("p (k c) -> p k c", k=KF), sh_down)

            def expert(l, slot, e, last):
                if last and e == 0:
                    return ring_ap(l, ("expert", E - 2)).rearrange("p (m n) -> p m n", m=3)
                return experts[:, slot, e]

            def all_tokens(l):
                shared_down(l)

                def four(i, last=False):
                    for e in range(4):
                        slot = e // 2
                        w = expert(l, slot, e % 2, last and slot == 1)
                        if e % 2 == 0:
                            pe.wait_ge(gu_landed[slot], i * 32 + (32 * (E // 4) * l + 32))
                            pe.wait_ge(wd_landed[slot], i * 16 + (16 * (E // 4) * l + 16))
                        for q in range(2):
                            ins = gate_or_up(q, w[:, q, :].rearrange("p (k c) -> p k c", k=KD))
                        ins.then_inc(a_gu[l], 1)
                        pe.wait_ge(a_h[l], i * 4 + (e + 1))
                        pe.wait_ge(a_yacc[l], i * 4 + (e + 1))
                        down(w[:, 2, :].rearrange("p (k c) -> p k c", k=KF), a_down[l])

                wait_item(pe, l, ("expert", E - 2))
                with pe.Fori(0, E // 4 - 1) as i:
                    four(i)
                four(E // 4 - 1, last=True)

            def compact(l):
                for t in (1, 0):
                    for k in range(KD):
                        o = (k % 4) * P
                        ins = nc.tensor.transpose(pb[:, UTOK_BANK[t] + k // 4, o:o + P], uT[:, k, t * P:(t + 1) * P], ident[:])
                    ins.then_inc(utok_done[l], 1)
                pe.wait_ge(sh_h, l + 1)
                pe.wait_ge(utok_ready[l], NT)
                xg, _, h_tok, hgT, weigh = scratch(l)

                def gather(n, read):
                    pe.wait_ge(choose_ready[l], n)
                    for k in range(KD):
                        if read is not None and k % 4 == 0:
                            pe.wait_ge(y_ready[l], read * 2 - 1 + k // 4)
                        ins = contract(pb[:, k // 4, (k % 4) * P:(k % 4 + 1) * P], lambda n: u_half[:, n // 2, n % 2, k, :],
                                       lambda n: choose[:, n // 2, :], 2 * NT)
                        if k % 4 == 3:
                            ins.then_inc(xg_done[l], 1)

                def up(n, slot, landed, last=False):
                    pe.wait_ge(xg0_ready[l], n)
                    pe.wait_ge(gu_landed[slot], landed)
                    if last:
                        wait_item(pe, l, ("expert", E - 2))
                    for k in range(KD):
                        if k == 4:
                            pe.wait_ge(xg1_ready[l], n)
                        for e in range(2):
                            ins = mm(pb[64 * e:64 * e + 64, 2, :], xg[:, k, CAP * e:CAP * (e + 1)],
                                     expert(l, slot, e, last)[:, 0:2, k * F:(k + 1) * F], start=(k == 0), stop=(k == KD - 1))
                    ins.then_inc(gu_free, 1)

                def turn(n, read):
                    pe.wait_ge(h_tok_ready[l], n)
                    pe.wait_ge(weigh_ready[l], n)
                    if read is not None:
                        pe.wait_ge(unchoose_ready[l], read)
                    for k in range(KF):
                        nc.tensor.transpose(pb[:, 3, k * P:(k + 1) * P], h_tok[:, k::KF], ident[:])
                    for t in range(NT):
                        ins = nc.tensor.transpose(pb[:, 3, S + t * P:S + (t + 1) * P], weigh[:, t, :], ident[:])
                    ins.then_inc(turned[l], 1)

                def scatter(n, parity, last=False):
                    pe.wait_ge(unchoose_ready[l], n)
                    for half in range(2):
                        pe.wait_ge(y_ready[l], n * 2 - 1 + half)
                        for t in range(NT):
                            for part in range(2):
                                ins = mm(pb[:, 4 + 2 * half + t, :], unchoose[:, parity, t * P:(t + 1) * P],
                                         y_half[:, part, half * 512:(half + 1) * 512], start=False, stop=True,
                                         skip_group_check=True)
                    if last:
                        ins.then_inc(scattered[l], 1)

                def down_pair(n, slot, landed, bank_read, last=False):
                    pe.wait_ge(hgT_ready[l], n)
                    pe.wait_ge(wd_landed[slot], landed)
                    for half in range(2):
                        pe.wait_ge((xg0_ready, xg1_ready)[half][l], bank_read)
                        for k in range(KF):
                            for e in range(2):
                                ins = mm(pb[64 * e:64 * e + 64, half, :], hgT[:, k, CAP * e:CAP * (e + 1)],
                                         expert(l, slot, e, last)[:, 2, k * D + half * 512:k * D + (half + 1) * 512],
                                         start=(k == 0), stop=(k == KF - 1))
                        ins.then_inc(wd_free if half else y0_done[l], 1)

                GU0, WD0 = 32 * (NP // 2) * l, 16 * (NP // 2) * l

                def step(i, q, first=False, last=False, before_last=False):
                    n = i * 2 + (q + 1)
                    if not last:
                        gather(n + 1, None if first else n - 1)
                    turn(n, None if first else n - 1)
                    if not first:
                        scatter(n - 1, (q + 1) % 2)
                    down_pair(n, q % 2, i * 16 + (WD0 + 16 * (q // 2 + 1)), n if last else n + 1, last)
                    if not last:
                        up(n + 1, (q + 1) % 2, i * 32 + (GU0 + 32 * ((q + 1) // 2 + 1)), before_last)

                gather(1, None)
                up(1, 0, GU0 + 32)
                shared_down(l)
                step(0, 0, first=True)
                with pe.Fori(0, (NP - 4) // 2) as i:
                    step(i, 1)
                    step(i, 2)
                for p in range(NP - 3, NP):
                    step(p // 2, p % 2, last=(p == NP - 1), before_last=(p == NP - 2))
                scatter(NP, (NP - 1) % 2, last=True)

            for l in range(L):
                if l == 0:
                    pe.wait_ge(first_landed, 16 * len(FIRST_LOADS))
                    pe.wait_ge(ones_ready, 1)
                    for j in range(4):
                        modulation(0, j)
                transpose_x(2 * l)
                pe.wait_ge(uT_lo, 2 * l + 1)
                pe.wait_ge(uT_hi, 2 * l + 1)
                if l == 0:
                    pe.wait_ge(consts_landed, 16 * len(CONST_LOADS))
                projections(l)
                attention(l)
                branches(l)
                mix_out(l)
                transpose_x(2 * l + 1)
                router(l)
                wait_item(pe, l, ("sh_gu", 0))
                w = ring_ap(l, ("sh_gu", 0)).rearrange("p (q k c) -> p q k c", q=2, k=KD)
                gate_or_up(0, w[:, 0]).then_inc(sh_gate_done, 1)
                places(l)
                gate_or_up(1, w[:, 1]).then_inc(sh_gu_done, 1)
                pe.wait_ge(flag_ready, l + 1)
                crowded = pe.value_load(flag[0:1, 0:1], min_val=0, max_val=1)
                with pe.If(crowded > 0):
                    all_tokens(l)
                with pe.Else():
                    compact(l)

        @block.scalar
        def _(act):
            def cp(dst, src):
                return nc.scalar.copy(dst, src)

            for dst, src in FIRST_LOADS:
                act.dma_start(dst, src).then_inc(first_landed, 16)
            act.wait_ge(c_landed, 16)
            nc.scalar.activation(silu_c[:, 1, :], silu_c[:, 0, :], ACT.Exp, scale=-1.0).then_inc(silu_exp, 1)
            act.wait_ge(acc_ready, 3)
            for dst, src in CONST_LOADS:
                act.dma_start(dst, src).then_inc(consts_landed, 16)

            def modulate_hi(n):
                act.wait_ge(turnT_ready, n + 1)
                for k in range(KD // 2, KD):
                    act.wait_ge(xT_done, KD // 2 * n + k // 2 + 1)
                    ins = nc.scalar.activation(uT[:, k, :], pb[:, k // 2, (k % 2) * S:(k % 2 + 1) * S], ACT.Identity,
                                               scale=turnT[:, 0, k:k + 1], bias=turnT[:, 1, k:k + 1])
                ins.then_inc(uT_hi, 1)

            def rotary(l, r):
                act.wait_ge(proj_done, NROPE * l + r + 1)
                if r >= 2:
                    act.wait_ge(rope_done, NROPE * l + r - 1)
                cp(raw[:, r % 2, :], pb[:, r % 2, 0:S]).then_inc(raw_ready, 1)

            def token_rows(l, g):
                for t in range(NT):
                    act.wait_ge(tok_done, NTOK * l + 2 * g + t + 1)
                    if g == 0:
                        cp(v_a[:, t, :], pb[:, 4 + t, 0:DH])
                        cp(ki_rows[:, t, :], pb[:, 4 + t, DH:DH + ID + IH]).then_inc(tok_read, 1)
                    else:
                        cp((v_b, v_c)[g - 1][:, t, :], pb[:, 4 + t, :]).then_inc(tok_read, 1)

            def indexer(l):
                act.wait_ge(kiT_done, l + 1)
                cp(kiT, pb[:, 7, S:2 * S]).then_inc(kiT_ready, 1)
                i = 0
                for t in range(NT):
                    for h in range(IH):
                        act.wait_ge(idx_done, NIDX * l + i + 1)
                        if i >= 2:
                            act.wait_ge(score_used, NIDX * l + i - 1)
                        nc.scalar.activation(relu[:, i % 2, 0:KEYS[t]], pb[:, 4 + i % 2, 0:KEYS[t]], ACT.Relu,
                                             scale=float(ID) ** -0.5).then_inc(relu_ready, 1)
                        i += 1

            def soft(l, i):
                act.wait_ge(max_ready, HC * l + i + 1)
                for t in range(NT):
                    a = lg[:, i % 4, KOFF[t]:KOFF[t] + KEYS[t]]
                    ins = nc.scalar.activation(a, a, ACT.Exp, bias=negmax[:, i % 4, t:t + 1],
                                               accum_out=esum[:, i % 4, t:t + 1])
                ins.then_inc(exp_done, 1)

            def probs_out(l, i):
                act.wait_ge(pt_done, HC * l + i + 1)
                if i >= 2:
                    act.wait_ge(pv_done, HC * l + i - 1)
                cp(pT[:, i % 2, :], pb[:, 2 + i % 2, 0:KALL]).then_inc(pt_ready, 1)

            def load_lent(l, j):
                n = lent.index((l, j))
                if n >= 3 and lent[n - 3][1] != "wout":
                    act.wait_ge(acc_ready, ada_order.index(lent[n - 3]) + 1)
                if l and j in OWN_ADA[:3]:
                    act.wait_ge(gu_free, NP * l)
                    act.wait_ge(wd_free, NP * l)
                a, s, _ = lent_buffer(l, j)
                if j == "wout":
                    src = w_out[l, :, SC:2 * SC].rearrange("(k p) c -> p k c", p=P)
                else:
                    src = ada_w[l, :, j * SC:(j + 1) * SC].rearrange("(p k) c -> p k c", k=KD)
                act.dma_start(a, src).then_inc(s, 16)

            def heads_out(l, hp):
                act.wait_ge(pv_done, HC * l + 2 * hp + 2)
                br = (1, 2, 0)[hp // 4]
                cp(oT[br][:, hp % 4, :], pb[:, 4 + hp % 2, 0:S]).then_inc(o_read, 1)

            def all_tokens(l):
                with act.Fori(0, E // 4) as i:
                    for e in range(4):
                        act.wait_ge(a_gu[l], i * 4 + (e + 1))
                        if e % 2:
                            act.sem_inc(gu_free, 1)
                        nc.scalar.activation(eh[:], pb[:, 0, :], ACT.Sigmoid).then_inc(a_exp[l], 1)
                        if e % 2:
                            act.wait_ge(a_down[l], i * 4 + (e + 1))
                            act.sem_inc(wd_free, 1)

            def compact(l):
                xg, sig, _, hgT, _ = scratch(l)
                for t in (1, 0):
                    act.wait_ge(utok_done[l], NT - t)
                    cp(u_half[:, t, 0].rearrange("p k c -> p (k c)"), pb[:, UTOK_BANK[t]:UTOK_BANK[t] + 2, :].rearrange("p b n -> p (b n)"))\
                        .then_inc(utok_hi[l], 1)

                def gathered(n):
                    act.wait_ge(xg_done[l], n * 2 - 1)
                    cp(xg[:, 0:4, :].rearrange("p k s -> p (k s)"), pb[:, 0, :]).then_inc(xg0_ready[l], 1)

                def step(i, q, last=False):
                    n = i * 2 + (q + 1)
                    act.wait_ge(gu_free, i * 2 + (NP * l + q + 1))
                    nc.scalar.activation(sig, pb[:, 2, 0:F], ACT.Sigmoid).then_inc(sig_ready[l], 1)
                    if not last:
                        gathered(n + 1)
                    act.wait_ge(turned[l], n)
                    cp(hgT.rearrange("p k s -> p (k s)"), pb[:, 3, 0:F]).then_inc(hgT_ready[l], 1)
                    for half in range(2):
                        act.wait_ge(*((wd_free, i * 2 + (NP * l + q + 1)) if half else (y0_done[l], n)))
                        if not half:
                            act.wait_ge(unchoose_ready[l], n)
                        nc.scalar.mul(y_half[:, 0, half * 512:(half + 1) * 512], pb[:, half, :], gate_of[:, 0:1])\
                            .then_inc(y_hi[l], 1)

                gathered(1)
                step(0, 0)
                with act.Fori(0, (NP - 4) // 2) as i:
                    step(i, 1)
                    step(i, 2)
                for p in range(NP - 3, NP):
                    step(p // 2, p % 2, last=(p == NP - 1))

            for l in range(L):
                modulate_hi(2 * l)
                r = 0
                ahead = sum(ada_with[l], [])
                for n, (blocks, tok) in enumerate(zip(BLOCKS, (None, 0, None, None, 1, None, None, 2))):
                    if ahead and (n < 3 or GROUPS[n] == "qc"):
                        load_lent(*ahead.pop(0))
                    for _ in range(blocks):
                        rotary(l, r)
                        r += 1
                    if tok is not None:
                        token_rows(l, tok)
                    if r == 11 and tok is None:
                        indexer(l)
                for j in OWN_ADA[:3]:
                    load_lent(l, j)
                for i in range(HC + 5):
                    if 3 <= i < HC + 3:
                        probs_out(l, i - 3)
                    if i < HC:
                        soft(l, i)
                    if i >= 6 and i % 2 == 0:
                        heads_out(l, (i - 6) // 2)
                for j in range(NGB):
                    act.wait_ge(gb_done, NGB * l + j + 1)
                    if j >= 2:
                        act.wait_ge(merged_done, NGB * l + j - 1)
                    nc.scalar.activation(sg[:, j % 2, :], pb[:, j % 2, 0:S], ACT.Sigmoid).then_inc(eg_ready, 1)
                    if j % EVERY == 0 and 3 <= j // EVERY + 2 <= len(OWN_ADA):
                        load_lent(l, (OWN_ADA + ("wout",))[j // EVERY + 2])
                modulate_hi(2 * l + 1)
                act.wait_ge(router_done, l + 1)
                nc.scalar.activation(rt[:, 0, :, :], pb[:, 2, 0:NT * E].rearrange("p (t e) -> p t e", t=NT), ACT.Exp,
                                     scale=-1.0).then_inc(er_ready, 1)
                act.wait_ge(sh_gate_done, l + 1)
                nc.scalar.activation(eh[:], pb[:, 0, :], ACT.Sigmoid).then_inc(sh_sig, 1)
                act.wait_ge(flag_ready, l + 1)
                crowded = act.value_load(flag[0:1, 0:1], min_val=0, max_val=1)
                with act.If(crowded > 0):
                    all_tokens(l)
                with act.Else():
                    compact(l)

        @block.vector
        def _(dve):
            v = nc.vector
            link = Chain(dve, dve_chain)
            v.memset(ones[:], 1.0).then_inc(ones_ready, 1)
            dve.wait_ge(silu_exp, 1)
            link(v.tensor_scalar(silu_c[:, 1, :], silu_c[:, 1, :], 1.0, None, ALU.add))
            link(v.reciprocal(silu_c[:, 2, :], silu_c[:, 1, :]))
            link(v.tensor_tensor(silu_c[:, 1, :], silu_c[:, 0, :], silu_c[:, 2, :], ALU.mult))

            evacuated = []

            def mod_evacuate(l, j):
                dve.wait_ge(mod_done, ada_order.index((l, j)) + 1)
                evacuated.append((l, j))
                piece, half = j // 2, j % 2
                if piece in (2, 5):
                    q = (piece - 2) // 3
                    if j == 4:
                        dve.wait_ge(gbias_landed, 32 * (l + 1))
                    a = g_bc[:, q, half * SC:(half + 1) * SC]
                    v.scalar_tensor_tensor(a, pb[:, 6, :], 1.0, a, ALU.add, ALU.add).then_inc(mod_read, 1)
                else:
                    q = (0, 1, None, 2, 3)[piece]
                    h = slice(64 * half, 64 * half + 64)
                    v.scalar_tensor_tensor(modT[h, l, q, :], pb[h, 7, q * KD:(q + 1) * KD], float(q % 2),
                                           adaT_bias[h, l, q, :], ALU.add, ALU.add).then_inc(mod_read, 1)

            def modulation_part(l, j, chunks):
                n = ada_order.index((l, j))
                if (l, j) in lent:
                    w, landed_sem, value = lent_buffer(l, j)
                else:
                    w = ring_ap(l, ("ada", j)).rearrange("p (k c) -> p k c", k=KD)
                a = acc[:, n % 2, :]
                if chunks[0] == 0:
                    if n >= 2 and ada_order[n - 2] not in evacuated:
                        mod_evacuate(*ada_order[n - 2])
                    if (l, j) in lent:
                        dve.wait_ge(landed_sem, value)
                    else:
                        wait_item(dve, l, ("ada", j))
                for k in chunks:
                    if k == 0:
                        ins = v.tensor_scalar(a, w[:, 0, :], silu_c[:, 1, 0:1], None, ALU.mult)
                    else:
                        ins = v.scalar_tensor_tensor(a, w[:, k, :], silu_c[:, 1, k:k + 1], a, ALU.mult, ALU.add)
                    if k < KD - 1:
                        link(ins)
                if chunks[-1] == KD - 1:
                    if n >= 2:
                        dve.wait_ge(mod_read, n - 1)
                    ins.then_inc(acc_ready, 1)

            def modulation(l, j):
                modulation_part(l, j, range(KD))

            def modulate(n):
                for k in range(KD // 2):
                    dve.wait_ge(xT_done, KD // 2 * n + k // 2 + 1)
                    ins = v.tensor_scalar(uT[:, k, :], pb[:, k // 2, (k % 2) * S:(k % 2 + 1) * S], turnT[:, 0, k:k + 1],
                                          turnT[:, 1, k:k + 1], ALU.mult, ALU.add)
                ins.then_inc(uT_lo, 1)

            def prepare_turn(n):
                if n:
                    dve.wait_ge(uT_hi, n)
                m = modT[:, n // 2, 2 * (n % 2):2 * (n % 2) + 2, :]
                if n == 0:
                    v.tensor_copy(turnT[:, 0, :], m[:, 1, :])
                    link(v.tensor_copy(turnT[:, 1, :], m[:, 0, :]))
                else:
                    g = lnT[:, (n - 1) // 2, (n - 1) % 2]
                    v.tensor_tensor(turnT[:, 0, :], g[:, 0, :], m[:, 1, :], ALU.mult)
                    link(v.tensor_tensor(turnT[:, 1, :], g[:, 1, :], m[:, 1, :], ALU.mult))
                    link(v.tensor_tensor(turnT[:, 1, :], turnT[:, 1, :], m[:, 0, :], ALU.add))
                v.tensor_copy(mark[:], turnT[:, 0, 0:1]).then_inc(turnT_ready, 1)

            ROPE_DST = [qT[0][:, b, :] for b in range(4)] + [kT[0][:, 0, :]] + [qiT[:, b, :] for b in range(2)]
            for br in (1, 2):
                ROPE_DST += [qT[br][:, b, :] for b in range(4)] + [kT[br][:, b, :] for b in range(4)]

            def rotary(l, r):
                q = 2 if r in (5, 6) else 0
                dve.wait_ge(raw_ready, NROPE * l + r + 1)
                if r:
                    dve.wait_ge(rope_done, NROPE * l + r)
                v.tensor_tensor(ropetmp[:, 0, :], raw[:, r % 2, :], rope[:, q, :], ALU.mult)
                dve.wait_ge(perm_done, NROPE * l + r + 1)
                link(v.tensor_tensor(ropetmp[:, 1, :], pb[:, 2 + r % 2, 0:S], rope[:, q + 1, :], ALU.mult))
                v.tensor_tensor(ROPE_DST[r], ropetmp[:, 0, :], ropetmp[:, 1, :], ALU.add).then_inc(rope_done, 1)

            def indexer_keys(l):
                dve.wait_ge(tok_read, NTOK * l + 2)
                for t in range(NT):
                    ins = v.bn_stats(stats[:, t, :], ki_rows[:, t, 0:ID])
                link(ins)
                for t in range(NT):
                    ins = v.bn_aggr(mv[:, t, :], stats[:, t, :])
                link(ins)
                v.tensor_scalar(ve, mv[:, :, 1], EPS, None, ALU.add).then_inc(var_ready, 1)
                dve.wait_ge(rstd_ready, 5 * l + 1)
                kn = ki_tmp
                for t in range(NT):
                    ins = v.tensor_scalar(kn[:, t, :], ki_rows[:, t, 0:ID], mv[:, t, 0:1], small[:, 4 + t:5 + t],
                                          ALU.subtract, ALU.mult)
                link(ins)
                for t in range(NT):
                    ins = v.tensor_tensor(kn[:, t, :], kn[:, t, :], ikgb[:, l, 0, :], ALU.mult)
                link(ins)
                for t in range(NT):
                    ins = v.tensor_tensor(kn[:, t, :], kn[:, t, :], ikgb[:, l, 1, :], ALU.add)
                link(ins)
                H = ID // 2
                x1, x2 = kn[:, :, 0:H], kn[:, :, H:ID]
                v.tensor_tensor(ki_prod[:, 0], x1, ropei_tok[:, 0], ALU.mult)
                v.tensor_tensor(ki_prod[:, 1], x2, ropei_tok[:, 1], ALU.mult)
                v.tensor_tensor(ki_prod[:, 2], x2, ropei_tok[:, 0], ALU.mult)
                link(v.tensor_tensor(ki_prod[:, 3], x1, ropei_tok[:, 1], ALU.mult))
                dst = ki_tok[:, 0:NT * P].rearrange("p (t c i) -> p t c i", t=NT, c=4)
                for c in range(4):
                    v.tensor_tensor(dst[:, :, c, 0:H], ki_prod[:, 0], ki_prod[:, 1], ALU.subtract)
                    ins = v.tensor_tensor(dst[:, :, c, H:ID], ki_prod[:, 2], ki_prod[:, 3], ALU.add)
                link(v.tensor_scalar(wi[:], ki_rows[:, :, ID:ID + IH], float(IH) ** -0.5, None, ALU.mult))
                ins = v.tensor_copy(mark[:], wi[:, 0, 0:1])
                ins.then_inc(ki_ready, 1)

            def indexer(l):
                i = 0
                for t in range(NT):
                    o = slice(KOFF[t], KOFF[t] + KEYS[t])
                    for h in range(IH):
                        dve.wait_ge(relu_ready, NIDX * l + i + 1)
                        other = masks[:, CAUSAL, o] if h == 0 else score[:, o]
                        v.scalar_tensor_tensor(score[:, o], relu[:, i % 2, 0:KEYS[t]], wi[:, t, h:h + 1], other,
                                               ALU.mult, ALU.add).then_inc(score_used, 1)
                        i += 1
                        dve.wait_ge(score_used, NIDX * l + i)

            def top_round(n):
                for t in range(NT):
                    o = slice(KOFF[t], KOFF[t] + KEYS[t])
                    ins = v.max(top8[:, t, n, :], score[:, o])
                link(ins)
                for t in range(NT):
                    o = slice(KOFF[t], KOFF[t] + KEYS[t])
                    ins = v.match_replace(score[:, o], top8[:, t, n, :], score[:, o], NEG)
                link(ins)

            def indexed_mask():
                link(v.tensor_scalar(masks[:, INDEXED, :], score, SELECTED, NEG, ALU.is_ge, ALU.mult))
                link(v.tensor_tensor(masks[:, INDEXED, :], masks[:, INDEXED, :], masks[:, CAUSAL, :], ALU.add))

            MASK_OF = (DILATED, CAUSAL, INDEXED)

            def logits(l, i):
                dve.wait_ge(s_done, HC * l + i + 1)
                if i >= 4:
                    dve.wait_ge(pt_done, HC * l + i - 3)
                v.scalar_tensor_tensor(lg[:, i % 4, :], pb[:, SCORE_BANK[i % 3], 0:KALL], SCALE,
                                       masks[:, MASK_OF[i // 8], :], ALU.mult, ALU.add).then_inc(s_read, 1)
                dve.wait_ge(s_read, HC * l + i + 1)
                for t in range(NT):
                    ins = v.tensor_reduce(negmax[:, i % 4, t:t + 1], lg[:, i % 4, KOFF[t]:KOFF[t] + KEYS[t]], AX.X, ALU.max,
                                          negate=True)
                ins.then_inc(max_ready, 1)

            def normalise(l, i):
                dve.wait_ge(exp_done, HC * l + i + 1)
                v.reciprocal(rden[:, i % 4, :], esum[:, i % 4, :]).then_inc(den_ready, 1)

            def sigmoid_den(a, link=link):
                link(v.tensor_scalar(a, a, 1.0, None, ALU.add))
                link(v.reciprocal(a, a))

            def merge(l):
                for j in range(NGB):
                    dve.wait_ge(eg_ready, NGB * l + j + 1)
                    a = sg[:, j % 2, :]
                    m = mergedT[:, j % KD, :]
                    if j < KD:
                        v.tensor_tensor(m, a, pb[:, 2 + j % 2, 0:S], ALU.mult).then_inc(merged_done, 1)
                    else:
                        link(v.tensor_tensor(a, a, pb[:, 2 + j % 2, 0:S], ALU.mult))
                        v.tensor_tensor(m, m, a, ALU.add).then_inc(merged_done, 1)
                    part = j % EVERY * 3
                    modulation_part(*own_ada[l][j // EVERY], range(part, min(part + 3, KD)))
                for a in own_ada[l][-2:]:
                    mod_evacuate(*a)
                dve.wait_ge(mod_read, ada_order.index(own_ada[l][-1]) + 1)
                dve.wait_ge(merged_done, NGB * (l + 1))

            PARTS = [(t, half) for half in range(2) for t in range(NT)]

            def norm(n, weighted=False):
                for t in range(NT):
                    for half in range(2):
                        o = slice(half * 512, half * 512 + 512)
                        if weighted:
                            gy = yacc[:, t, o]
                        else:
                            dve.wait_ge(y_done, 4 * (n // 2) + 2 * t + half + 1)
                            gy = acc[:, half, :]
                            link(v.tensor_tensor(gy, pb[:, 4 + 2 * half + t, :], g_bc[:, n % 2, o], ALU.mult))
                        link(v.scalar_tensor_tensor(xs[:, t, o], xs[:, t, o], ALPHA, gy, ALU.mult, ALU.add))
                        link(v.bn_stats(stats[:, 2 * t + half, :], xs[:, t, o]))
                    link(v.bn_aggr(mv[:, t, :], stats[:, 2 * t:2 * t + 2, :]))
                    v.tensor_scalar(ve[:, t:t + 1], mv[:, t, 1:2], EPS, None, ALU.add).then_inc(var_ready, 1)
                    dve.wait_ge(rstd_ready, 5 * (n // 2) + 2 + 2 * (n % 2) + t)
                    v.tensor_scalar(xs[:, t, :], xs[:, t, :], mv[:, t, 0:1], rs[:, t:t + 1], ALU.subtract, ALU.mult)\
                        .then_inc(xn_ready, 1)
                dve.wait_ge(xn_ready, 2 * n + 2)

            def affine(n):
                wait_item(dve, n // 2, ("ln", n % 2))
                if n < 2 * L - 1:
                    dve.wait_ge(xT_done, KD // 2 * (n + 2))
                ln_bc = ring_ap(n // 2, ("ln", n % 2)).rearrange("p (m d) -> p m d", m=2)
                first = 1 if n == 2 * L - 1 else 0
                for m, op in enumerate((ALU.mult, ALU.add)):
                    for t in range(first, NT):
                        ins = v.tensor_tensor(xs[:, t, :], xs[:, t, :], ln_bc[:, m, :], op)
                    if m == 0:
                        link(ins)
                ins.then_inc(norm_done, 1)
                dve.wait_ge(norm_done, n + 1)

            def route(l):
                dve.wait_ge(er_ready, l + 1)
                sc, biased, gm, w = rt[:, 0], rt[:, 1], rt[:, 2], rt[:, 3]
                sigmoid_den(sc)
                for t in range(NT):
                    ins = v.tensor_tensor(biased[:, t, :], sc[:, t, :], rbias[:, l, :], ALU.add)
                link(ins)
                G = 8
                for t in range(NT):
                    for g in range(G):
                        ins = v.max(top8[:, t, g, :], biased[:, t, g * G:(g + 1) * G])
                link(ins)
                gs = gscore
                link(v.tensor_tensor(gs[:, 0], top8[:, :, :, 0], top8[:, :, :, 1], ALU.add))
                for t in range(NT):
                    ins = v.max(gs[:, 1, t, :], gs[:, 0, t, :])
                link(ins)
                link(v.memset(gs[:, 1, :, 4:8], -NEG))
                for t in range(NT):
                    ins = v.match_replace(gs[:, 2, t, :], gs[:, 1, t, :], gs[:, 0, t, :], NEG)
                link(ins)
                link(v.tensor_scalar(gs[:, 2], gs[:, 2], SELECTED, NEG, ALU.is_ge, ALU.mult))
                for g in range(G):
                    for t in range(NT):
                        ins = v.tensor_scalar(gm[:, t, g * G:(g + 1) * G], biased[:, t, g * G:(g + 1) * G],
                                              gs[:, 2, t, g:g + 1], None, ALU.add)
                link(ins)
                for t in range(NT):
                    ins = v.max(top8[:, t, 0, :], gm[:, t, :])
                link(ins)
                for t in range(NT):
                    ins = v.match_replace(w[:, t, :], top8[:, t, 0, :], gm[:, t, :], 2 * NEG)
                link(ins)
                sel = rt[:, 4]
                v.tensor_scalar(sel, w, 1.5 * NEG, None, ALU.is_lt).then_inc(chosen, 1)
                dve.wait_ge(chosen, l + 1)
                link(v.tensor_tensor(w, sel, sc, ALU.mult))
                link(v.tensor_reduce(gsum[:, 0, :], w, AX.X, ALU.add))
                link(v.reciprocal(gsum[:, 1, :], gsum[:, 0, :]))
                for t in range(NT):
                    ins = v.tensor_scalar(gates[:, t, :], w[:, t, :], gsum[:, 1, t:t + 1], 2.5, ALU.mult, ALU.mult)
                link(ins)

            def ffn_h(link, done, up_done=None, value=None):
                a = eh[:]
                link(v.tensor_tensor(a, a, pb[:, 0, :], ALU.mult))
                if up_done is not None:
                    dve.wait_ge(up_done, value)
                v.tensor_tensor(hT.rearrange("p k n -> p (k n)"), a, pb[:, 1, :], ALU.mult).then_inc(done, 1)

            def crowding(l):
                sel = rt[:, 4]
                dve.wait_ge(placed, l + 1)
                link(v.scalar_tensor_tensor(place[:], pb[:, 3, 0:2 * E].rearrange("p (t e) -> p t e", t=NT), 1.0, sel,
                                            ALU.add, ALU.mult))
                v.tensor_scalar(place[:], place[:], -1.0, None, ALU.add)
                link(v.tensor_reduce(gsum[:, 0, 0:1], pb[:, 3, 2 * E:3 * E], AX.X, ALU.max))
                v.tensor_scalar(flag[:], gsum[:, 0, 0:1], float(LIMIT), None, ALU.is_gt).then_inc(flag_ready, 1)
                dve.wait_ge(flag_ready, l + 1)

            def column(a, t, e):
                return a[:].rearrange("p t e -> p (t e)")[:, bass.ds(e + t * E, 1)]

            def all_tokens(l):
                link = Chain(dve, a_chain[l])
                dve.wait_ge(sh_down, l + 1)
                for t, half in PARTS:
                    ins = v.tensor_copy(yacc[:, t, half * 512:(half + 1) * 512], pb[:, 4 + 2 * half + t, :])
                ins.then_inc(a_yacc[l], 1)
                K = 1
                with dve.Fori(0, E // 4) as i:
                    for e in range(4):
                        link.turn = i * (4 * K)
                        dve.wait_ge(a_exp[l], i * 4 + (e + 1))
                        ffn_h(link, a_h[l])
                        dve.wait_ge(a_down[l], i * 4 + (e + 1))
                        dve.wait_ge(a_yacc[l], i * 4 + (e + 1))
                        for t, half in PARTS:
                            a = yacc[:, t, half * 512:(half + 1) * 512]
                            ins = v.scalar_tensor_tensor(a, pb[:, 4 + 2 * half + t, :], column(gates, t, i * 4 + e), a,
                                                         ALU.mult, ALU.add)
                        ins.then_inc(a_yacc[l], 1)
                    assert link.n == 4 * K
                dve.wait_ge(a_yacc[l], E + 1)
                for t, half in PARTS:
                    o = slice(half * 512, half * 512 + 512)
                    ins = v.tensor_tensor(yacc[:, t, o], yacc[:, t, o], g_bc[:, 1, o], ALU.mult)
                ins.then_inc(yg_ready, 1)

            def compact(l):
                link = Chain(dve, c_chain[l])
                xg, sig, h_tok, _, weigh = scratch(l)
                def choice(e0, gathered):
                    if gathered is not None:
                        dve.wait_ge(xg_done[l], gathered)
                    for t in range(NT):
                        for e in range(2):
                            ins = v.tensor_scalar(choose[:, t, CAP * e:CAP * (e + 1)], slots[:], column(place, t, e0 + e), None,
                                                  ALU.is_equal)
                    ins.then_inc(choose_ready[l], 1)

                def weights(e0, read):
                    if read is not None:
                        dve.wait_ge(turned[l], read)
                    for t in range(NT):
                        for e in range(2):
                            ins = v.tensor_scalar(weigh[:, t, CAP * e:CAP * (e + 1)], slots[:], column(place, t, e0 + e),
                                                  column(gates, t, e0 + e), ALU.is_equal, ALU.mult)
                    ins.then_inc(weigh_ready[l], 1)

                def gathered(n):
                    dve.wait_ge(xg_done[l], n * 2)
                    v.tensor_copy(xg[:, 4:8, :].rearrange("p k s -> p (k s)"), pb[:, 1, :]).then_inc(xg1_ready[l], 1)

                def step(i, q, turn=0):
                    n, e0 = i * 2 + (q + 1), i * 4 + 2 * q
                    dve.wait_ge(sig_ready[l], n)
                    link(v.tensor_tensor(sig, sig, pb[:, 2, 0:F], ALU.mult))
                    v.tensor_tensor(h_tok, sig, pb[:, 2, F:2 * F], ALU.mult).then_inc(h_tok_ready[l], 1)
                    if turn < NP - 1:
                        gathered(n + 1)
                    if turn < NP - 2:
                        choice(e0 + 4, None)
                    dve.wait_ge(hgT_ready[l], n)
                    v.tensor_reduce(gate_of[:], pb[:, 3, F:2 * F], AX.X, ALU.add)
                    v.tensor_scalar(unchoose[:, q % 2, :], pb[:, 3, F:2 * F], 0.0, None, ALU.is_gt).then_inc(unchoose_ready[l], 1)
                    if turn < NP - 1:
                        weights(e0 + 2, n)
                    for half in range(2):
                        dve.wait_ge(y_hi[l], i * 4 + (2 * q + half + 1))
                        o = slice(half * 512, (half + 1) * 512)
                        v.scalar_tensor_tensor(y_half[:, 1, o], pb[:, half, :], gate_of[:, 0:1], y_half[:, 0, o].bitcast(F32),
                                               ALU.mult, ALU.subtract).then_inc(y_ready[l], 1)

                for t in (1, 0):
                    dve.wait_ge(utok_hi[l], NT - t)
                    v.tensor_tensor(u_half[:, t, 1].rearrange("p k c -> p (k c)"),
                                    pb[:, UTOK_BANK[t]:UTOK_BANK[t] + 2, :].rearrange("p b n -> p (b n)"),
                                    u_half[:, t, 0].bitcast(F32).rearrange("p k c -> p (k c)"), ALU.subtract).then_inc(utok_ready[l], 1)
                    if t == 1:
                        choice(0, None)
                weights(0, None)
                gathered(1)
                choice(2, 2)
                step(0, 0)
                n0 = link.n
                with dve.Fori(0, (NP - 4) // 2) as i:
                    link.turn = i * (2 * n0)
                    step(i, 1)
                    step(i, 2)
                assert link.n == 3 * n0
                link.turn, link.n = 0, n0 * (NP - 3)
                for p in range(NP - 3, NP):
                    step(p // 2, p % 2, turn=p)
                dve.wait_ge(scattered[l], 1)
                for t, half in PARTS:
                    o = slice(half * 512, half * 512 + 512)
                    ins = v.tensor_tensor(yacc[:, t, o], pb[:, 4 + 2 * half + t, :], g_bc[:, 1, o], ALU.mult)
                ins.then_inc(yg_ready, 1)

            for l in range(L):
                if l == 0:
                    for j in range(4):
                        modulation(0, j)
                    for j in (2, 3):
                        mod_evacuate(0, j)
                    dve.wait_ge(mod_read, 4)
                    prepare_turn(0)
                modulate(2 * l)
                if l:
                    affine(2 * l - 1)
                r = rounds = 0
                for n, blocks in enumerate(BLOCKS):
                    for b in range(max(blocks, 1)):
                        if blocks:
                            rotary(l, r)
                            r += 1
                        if b < 3:
                            for a in ada_with[l][n]:
                                modulation_part(*a, range(3 * b, min(3 * b + 3, KD)))
                        if r > 11 and blocks and rounds < TOPK_ROUNDS:
                            top_round(rounds)
                            rounds += 1
                    if GROUPS[n] == "small":
                        indexer_keys(l)
                    if GROUPS[n] == "qb":
                        indexer(l)
                indexed_mask()
                for i in range(HC + 1):
                    if i < HC:
                        logits(l, i)
                    if i:
                        normalise(l, i - 1)
                merge(l)
                prepare_turn(2 * l + 1)
                norm(2 * l)
                modulate(2 * l + 1)
                affine(2 * l)
                if l < L - 1:
                    prepare_turn(2 * l + 2)
                route(l)
                crowding(l)
                dve.wait_ge(sh_sig, l + 1)
                ffn_h(link, sh_h, sh_gu_done, l + 1)
                dve.wait_ge(sh_h, l + 1)
                crowded = dve.value_load(flag[0:1, 0:1], min_val=0, max_val=1)
                with dve.If(crowded > 0):
                    all_tokens(l)
                with dve.Else():
                    compact(l)
                dve.wait_ge(yg_ready, l + 1)
                norm(2 * l + 1, weighted=True)
            affine(2 * L - 1)


def constants(S):
    import numpy as np
    P, NEG = 128, np.float32(-1.0e30)
    NT = S // P

    def rope_tables(dim):
        inv = np.float32(10000.0) ** (-np.arange(0, dim, 2, dtype=np.float32) / np.float32(dim))
        ang = np.arange(S, dtype=np.float32)[:, None] * inv[None, :].astype(np.float32)
        return np.cos(ang, dtype=np.float32), np.sin(ang, dtype=np.float32)

    rope = np.zeros((P, 4, S), np.float32)
    perm = np.zeros((P, 2, P), np.float32)
    for n, dim in enumerate((64, 32)):
        c, s = rope_tables(dim)
        h = dim // 2
        for p in range(P):
            rope[p, 2 * n], rope[p, 2 * n + 1] = c[:, p % h], s[:, p % h]
            if p % dim < h:
                perm[p + h, n, p] = -1.0
            else:
                perm[p - h, n, p] = 1.0
    c, s = rope_tables(32)
    ropei = np.stack([c.reshape(NT, P, 16), s.reshape(NT, P, 16)]).transpose(2, 0, 1, 3)
    masks = np.full((P, 2, P + S), NEG, np.float32)
    for t, off in ((0, 0), (1, P)):
        q = (t * P + np.arange(P))[:, None]
        k = np.arange(P * (t + 1))[None, :]
        d = q - k
        masks[:, 0, off:off + P * (t + 1)] = np.where(d >= 0, np.float32(0), NEG)
        count = np.zeros(d.shape, np.int64)
        for window, dil in ((128, 1), (512, 4), (2048, 16)):
            count += (d >= 0) & (d <= window) & (d % dil == 0)
        masks[:, 1, off:off + P * (t + 1)] = np.where(count > 0, np.log(np.maximum(count, 1)), NEG)
    return {"ident": np.eye(P, dtype=np.float32), "perm": perm, "rope": rope,
            "ropei_tok": np.ascontiguousarray(ropei), "masks": masks,
            "before": np.triu(np.ones((P, P), np.float32), 1),
            "slots": np.tile(np.arange(64, dtype=np.float32), (P, 1))}


def kernel(**inputs):
    import numpy as _np
    import concourse.bacc as _bacc
    from concourse import mybir as _mybir
    from concourse.bass_utils import run_bass_kernel_spmd as _run

    g = {n: _np.asarray(a) for n, a in inputs.items()}
    L, D, KD = g["w_in"].shape[0], g["w_in"].shape[1], 8
    c = constants(g["x"].shape[1])
    ada_b = g["ada_b"].reshape(L, 6, 128, KD)
    ln_gb = _np.stack([_np.stack([g["ln1_g"], g["ln1_b"]], 1), _np.stack([g["ln2_g"], g["ln2_b"]], 1)], 1)
    arrays = {
        "x": g["x"][0], "cT": g["c"].reshape(128, KD), "ada_w": g["ada_w"],
        "adaT_b": _np.ascontiguousarray(ada_b[:, (0, 1, 3, 4)].transpose(2, 0, 1, 3)), "ada_b": g["ada_b"],
        "w_in": g["w_in"], "ik_gb": _np.stack([g["ik_norm_g"], g["ik_norm_b"]], 1),
        "w_br_a": g["w_br_a"], "w_br_b": g["w_br_b"], "w_br_c": g["w_br_c"], "w_out": g["w_out"],
        "ln_gb": ln_gb,
        "w_router": g["w_router"], "router_bias": g["router_bias"],
        "w_gate": g["w_gate"], "w_up": g["w_up"], "w_down": g["w_down"],
        "ws_gate": g["ws_gate"], "ws_up": g["ws_up"], "ws_down": g["ws_down"],
        "ident_c": c["ident"], "perm_c": c["perm"], "rope_c": c["rope"], "ropei_tok_c": c["ropei_tok"], "mask_c": c["masks"],
        "lnT_c": _np.ascontiguousarray(ln_gb.reshape(L, 2, 2, 128, KD).transpose(3, 0, 1, 2, 4)),
        "before_c": c["before"], "slot_c": c["slots"],
    }
    nc = _bacc.Bacc("TRN2", target_bir_lowering=False, num_devices=1)
    given, args = {}, []
    for name, a in arrays.items():
        a = _np.ascontiguousarray(a)
        given[f"in_{name}"] = a
        args.append(nc.dram_tensor(f"in_{name}", a.shape, _mybir.dt.from_np(a.dtype), kind="ExternalInput").ap())
    args.append(nc.dram_tensor("out_0", g["x"].shape[1:], F32, kind="ExternalOutput").ap())
    build(nc, *args)
    r = _run(nc, [given], core_ids=[0])
    return r.results[0]["out_0"][None]
```
